# Optimizing a Trainium2 kernel written in Bass

```python
import jax, jax.numpy as jnp
from jax import lax
import numpy as np
import math

D_MODEL = 1024
BATCH = 1
SEQ = 512
DEPTH = 2

N_HEADS = 16
HEAD_DIM = 64
ATTN_WIDTH = N_HEADS * HEAD_DIM
DILATED_PATTERNS = ((128, 1), (512, 4), (2048, 16))
N_GROUPS = len(DILATED_PATTERNS)
FOX_Q_BLOCK = 128
ROT_DIM = HEAD_DIM // 4
ROPE_THETA = 500000.0
D_FF = -(-8 * D_MODEL // (3 * 256)) * 256
RMS_EPS = 1e-6
NEG_INF = -1e30
N_MIXERS = 2
N_A_LAYERS = (DEPTH + 1) // 2
N_B_LAYERS = DEPTH // 2


def rmsnorm(x, g):
    xf = x.astype(jnp.float32)
    y = xf * lax.rsqrt(jnp.mean(xf * xf, axis=-1, keepdims=True) + RMS_EPS) * g.astype(jnp.float32)
    return y.astype(x.dtype)

def partial_rotary(t, pos):
    half = ROT_DIM // 2
    inv_freq = ROPE_THETA ** (-jnp.arange(half, dtype=jnp.float32) * 2.0 / ROT_DIM)
    ang = pos[:, None] * inv_freq[None, :]
    cos = jnp.cos(ang)[None, :, None, :]
    sin = jnp.sin(ang)[None, :, None, :]
    t1 = t[..., :half].astype(jnp.float32)
    t2 = t[..., half:ROT_DIM].astype(jnp.float32)
    rot = jnp.concatenate([t1 * cos - t2 * sin, t2 * cos + t1 * sin], axis=-1).astype(t.dtype)
    return jnp.concatenate([rot, t[..., ROT_DIM:]], axis=-1)

def dilated_band_attention(q, k, v, dil, steps):
    B, S, H, D = q.shape
    L = S // dil
    blk = steps
    nb = -(-L // blk)
    Lp = nb * blk

    def by_stride(t):
        t = t.reshape(B, L, dil, H, D).transpose(0, 2, 1, 3, 4)
        return jnp.pad(t, ((0, 0), (0, 0), (0, Lp - L), (0, 0), (0, 0)))

    def band(t):
        tp = jnp.pad(t, ((0, 0), (0, 0), (blk, 0), (0, 0), (0, 0))).reshape(B, dil, nb + 1, blk, H, D)
        return jnp.concatenate([tp[:, :, :-1], tp[:, :, 1:]], axis=3)

    qb = by_stride(q).reshape(B, dil, nb, blk, H, D)
    kb = band(by_stride(k))
    vb = band(by_stride(v))

    s = jnp.einsum('bcnihd,bcnjhd->bcnhij', qb, kb).astype(jnp.float32) * (D ** -0.5)
    i = jnp.arange(blk)[:, None]
    j = jnp.arange(2 * blk)[None, :]
    diff = i + blk - j
    key_step = (jnp.arange(nb)[:, None] - 1) * blk + jnp.arange(2 * blk)[None, :]
    valid = ((diff >= 0) & (diff <= steps))[None, :, :] & (key_step >= 0)[:, None, :]
    s = jnp.where(valid[None, None, :, None, :, :], s, NEG_INF)

    m = jnp.max(s, axis=-1, keepdims=True)
    p = jnp.exp(s - m)
    den = jnp.sum(p, axis=-1, keepdims=True)
    o = jnp.einsum('bcnhij,bcnjhd->bcnihd', p / den, vb.astype(jnp.float32))
    lse = (m + jnp.log(den))[..., 0]

    o = o.reshape(B, dil, Lp, H, D)[:, :, :L].transpose(0, 2, 1, 3, 4).reshape(B, S, H, D)
    lse = lse.transpose(0, 1, 2, 4, 3).reshape(B, dil, Lp, H)[:, :, :L].transpose(0, 2, 1, 3).reshape(B, S, H)
    return o, lse

def dilated_mixer(h, w_in, w_out):
    B, S, _ = h.shape
    proj = (h @ w_in).reshape(B, S, N_GROUPS, 3, N_HEADS, HEAD_DIM)
    pos = jnp.arange(S, dtype=jnp.float32)
    outs, lses = [], []
    for g, (window, dil) in enumerate(DILATED_PATTERNS):
        q = partial_rotary(proj[:, :, g, 0], pos)
        k = partial_rotary(proj[:, :, g, 1], pos)
        v = proj[:, :, g, 2]
        o, lse = dilated_band_attention(q, k, v, dil, window // dil)
        outs.append(o)
        lses.append(lse)
    wts = jax.nn.softmax(jnp.stack(lses, axis=0), axis=0)
    o = jnp.einsum('gbsh,gbshd->bshd', wts, jnp.stack(outs, axis=0))
    return o.reshape(B, S, ATTN_WIDTH).astype(h.dtype) @ w_out

def forgetting_mixer(h, w_in, b_f, w_out):
    B, S, _ = h.shape
    proj = h @ w_in
    qkv = proj[..., :3 * ATTN_WIDTH].reshape(B, S, 3, N_HEADS, HEAD_DIM)
    q, k, v = qkv[:, :, 0], qkv[:, :, 1], qkv[:, :, 2]
    log_f = jax.nn.log_sigmoid(proj[..., 3 * ATTN_WIDTH:].astype(jnp.float32) + b_f.astype(jnp.float32))
    c = lax.cumsum(log_f, axis=1)
    nq = S // FOX_Q_BLOCK
    qb = q.reshape(B, nq, FOX_Q_BLOCK, N_HEADS, HEAD_DIM).transpose(1, 0, 2, 3, 4)
    cqb = c.reshape(B, nq, FOX_Q_BLOCK, N_HEADS).transpose(1, 0, 3, 2)
    ck = c.transpose(0, 2, 1)
    key_pos = jnp.arange(S)
    vf = v.astype(jnp.float32)
    scale = HEAD_DIM ** -0.5

    def block(args):
        qi, ci, n = args
        s = jnp.einsum('bihd,bjhd->bhij', qi, k).astype(jnp.float32) * scale
        s = s + ci[..., None] - ck[:, :, None, :]
        qpos = n * FOX_Q_BLOCK + jnp.arange(FOX_Q_BLOCK)
        s = jnp.where(key_pos[None, :] <= qpos[:, None], s, NEG_INF)
        p = jax.nn.softmax(s, axis=-1)
        return jnp.einsum('bhij,bjhd->bihd', p, vf)

    o = lax.map(block, (qb, cqb, jnp.arange(nq)))
    o = o.transpose(1, 0, 2, 3, 4).reshape(B, S, ATTN_WIDTH).astype(h.dtype)
    return o @ w_out

def swiglu(h, w_gu, w_down):
    gu = h @ w_gu
    g, u = gu[..., :D_FF], gu[..., D_FF:]
    return (jax.nn.silu(g) * u) @ w_down

def first_inputs(seed: int = 0) -> dict:
    key = jax.random.key(seed)
    ks = jax.random.split(key, 13)
    f32 = jnp.float32
    x = jax.random.normal(ks[0], (BATCH, SEQ, D_MODEL), f32)
    a_norm = 1.0 + 0.02 * jax.random.normal(ks[1], (N_A_LAYERS, D_MODEL), f32)
    a_w_in = jax.random.normal(ks[2], (N_A_LAYERS, D_MODEL, N_GROUPS * 3 * ATTN_WIDTH), f32) * D_MODEL ** -0.5
    a_w_out = jax.random.normal(ks[3], (N_A_LAYERS, ATTN_WIDTH, D_MODEL), f32) * ATTN_WIDTH ** -0.5
    b_norm = 1.0 + 0.02 * jax.random.normal(ks[4], (N_B_LAYERS, D_MODEL), f32)
    b_w_in = jax.random.normal(ks[5], (N_B_LAYERS, D_MODEL, 3 * ATTN_WIDTH + N_HEADS), f32) * D_MODEL ** -0.5
    b_f = jnp.linspace(1.0, 6.0, N_HEADS, dtype=f32)[None, :] + 0.1 * jax.random.normal(ks[6], (N_B_LAYERS, N_HEADS), f32)
    b_w_out = jax.random.normal(ks[7], (N_B_LAYERS, ATTN_WIDTH, D_MODEL), f32) * ATTN_WIDTH ** -0.5
    ffn_norm = 1.0 + 0.02 * jax.random.normal(ks[8], (DEPTH, D_MODEL), f32)
    ffn_w_gu = jax.random.normal(ks[9], (DEPTH, D_MODEL, 2 * D_FF), f32) * D_MODEL ** -0.5
    ffn_w_down = jax.random.normal(ks[10], (DEPTH, D_FF, D_MODEL), f32) * D_FF ** -0.5
    final_norm = 1.0 + 0.02 * jax.random.normal(ks[11], (D_MODEL,), f32)
    return {"x": x, "a_norm": a_norm, "a_w_in": a_w_in, "a_w_out": a_w_out,
            "b_norm": b_norm, "b_w_in": b_w_in, "b_f": b_f, "b_w_out": b_w_out,
            "ffn_norm": ffn_norm, "ffn_w_gu": ffn_w_gu, "ffn_w_down": ffn_w_down,
            "final_norm": final_norm}

def first_block(x, a_norm, a_w_in, a_w_out, b_norm, b_w_in, b_f, b_w_out,
              ffn_norm, ffn_w_gu, ffn_w_down, final_norm):
    h = x
    for i in range(DEPTH):
        j = i // N_MIXERS
        if i % N_MIXERS == 0:
            h = h + dilated_mixer(rmsnorm(h, a_norm[j]), a_w_in[j], a_w_out[j])
        else:
            h = h + forgetting_mixer(rmsnorm(h, b_norm[j]), b_w_in[j], b_f[j], b_w_out[j])
        h = h + swiglu(rmsnorm(h, ffn_norm[i]), ffn_w_gu[i], ffn_w_down[i])
    return rmsnorm(h, final_norm)


N_LRU = (DEPTH + 1) // 2
N_RET = DEPTH // 2

D_RNN = 3 * D_MODEL // 2
N_GATE_BLOCKS = 16
BLOCK_W = D_RNN // N_GATE_BLOCKS
CONV_W = 4
C_RG = 8.0

RET_HEADS = D_MODEL // 256
QK_HEAD = 256
V_HEAD = 2 * QK_HEAD
QK_DIM = RET_HEADS * QK_HEAD
V_DIM = RET_HEADS * V_HEAD
CHUNK = 128
ROPE_BASE = 10000.0

GN_EPS = 1e-5


def rms_norm(x, g):
    xf = x.astype(jnp.float32)
    y = xf * lax.rsqrt(jnp.mean(xf * xf, axis=-1, keepdims=True) + RMS_EPS)
    return (y * g.astype(jnp.float32)).astype(x.dtype)

def causal_depthwise_conv(x, w, b):
    s = x.shape[1]
    xp = jnp.pad(x, ((0, 0), (CONV_W - 1, 0), (0, 0)))
    y = b
    for k in range(CONV_W):
        y = y + xp[:, k:k + s] * w[k]
    return y

def _lin_rec_combine(e1, e2):
    a1, b1 = e1
    a2, b2 = e2
    return a1 * a2, a2 * b1 + b2

def rglru_mixer(h, w_in, conv_w, conv_b, w_a, b_a, w_x, b_x, lam, w_out):
    bsz, s, _ = h.shape
    u = h @ w_in
    xb, gate = u[..., :D_RNN], u[..., D_RNN:]
    xb = causal_depthwise_conv(xb, conv_w, conv_b)
    xblk = xb.reshape(bsz, s, N_GATE_BLOCKS, BLOCK_W)
    r = jax.nn.sigmoid(jnp.einsum('bsnc,ncd->bsnd', xblk, w_a).reshape(bsz, s, D_RNN) + b_a)
    i = jax.nn.sigmoid(jnp.einsum('bsnc,ncd->bsnd', xblk, w_x).reshape(bsz, s, D_RNN) + b_x)
    log_a = -C_RG * r.astype(jnp.float32) * jax.nn.softplus(-lam.astype(jnp.float32))
    a = jnp.exp(log_a)
    bt = jnp.sqrt(-jnp.expm1(2.0 * log_a)) * (i * xb).astype(jnp.float32)
    _, hseq = lax.associative_scan(_lin_rec_combine, (a, bt), axis=1)
    y = hseq.astype(h.dtype) * jax.nn.silu(gate)
    return y @ w_out

def apply_rotary(x, cos, sin):
    half = x.shape[-1] // 2
    x1, x2 = x[..., :half], x[..., half:]
    c = cos[None, :, None, :]
    s_ = sin[None, :, None, :]
    return jnp.concatenate([x1 * c - x2 * s_, x2 * c + x1 * s_], axis=-1)

def retention_mixer(h, w_in, w_out, cos, sin):
    bsz, s, _ = h.shape
    n_chunks = s // CHUNK
    u = h @ w_in
    q = u[..., :QK_DIM].reshape(bsz, s, RET_HEADS, QK_HEAD).astype(jnp.float32)
    k = u[..., QK_DIM:2 * QK_DIM].reshape(bsz, s, RET_HEADS, QK_HEAD).astype(jnp.float32)
    v = u[..., 2 * QK_DIM:2 * QK_DIM + V_DIM].reshape(bsz, s, RET_HEADS, V_HEAD).astype(jnp.float32)
    gate = u[..., 2 * QK_DIM + V_DIM:]
    q = apply_rotary(q, cos, sin)
    k = apply_rotary(k, cos, sin) * (QK_HEAD ** -0.5)

    def to_chunks(t):
        return t.reshape(bsz, n_chunks, CHUNK, RET_HEADS, t.shape[-1]).transpose(1, 0, 3, 2, 4)

    qc, kc, vc = to_chunks(q), to_chunks(k), to_chunks(v)

    log_g = jnp.log(1.0 - jnp.exp2(-5.0 - jnp.arange(RET_HEADS, dtype=jnp.float32)))
    idx = jnp.arange(CHUNK, dtype=jnp.float32)
    diff = idx[:, None] - idx[None, :]
    dmask = jnp.where(diff[None] >= 0, jnp.exp(jnp.maximum(diff, 0.0)[None] * log_g[:, None, None]), 0.0)
    q_decay = jnp.exp((idx[None, :] + 1.0) * log_g[:, None])[..., None]
    k_decay = jnp.exp((CHUNK - 1.0 - idx[None, :]) * log_g[:, None])[..., None]
    chunk_decay = jnp.exp(CHUNK * log_g)[:, None, None]

    def step(state, inp):
        qi, ki, vi = inp
        scores = jnp.einsum('bhqd,bhkd->bhqk', qi, ki) * dmask
        inner = jnp.einsum('bhqk,bhke->bhqe', scores, vi)
        cross = jnp.einsum('bhqd,bhde->bhqe', qi * q_decay, state)
        new_state = state * chunk_decay + jnp.einsum('bhkd,bhke->bhde', ki * k_decay, vi)
        return new_state, inner + cross

    state0 = jnp.zeros((bsz, RET_HEADS, QK_HEAD, V_HEAD), jnp.float32)
    _, out = lax.scan(step, state0, (qc, kc, vc))
    out = out.transpose(1, 0, 3, 2, 4).reshape(bsz, s, RET_HEADS, V_HEAD)
    mu = jnp.mean(out, axis=-1, keepdims=True)
    var = jnp.mean(jnp.square(out - mu), axis=-1, keepdims=True)
    out = ((out - mu) * lax.rsqrt(var + GN_EPS)).reshape(bsz, s, V_DIM).astype(h.dtype)
    y = out * jax.nn.silu(gate)
    return y @ w_out

def second_inputs(seed: int = 0) -> dict:
    key = jax.random.key(seed)
    ks = jax.random.split(key, 16)
    f32 = jnp.float32

    def nrm(k, shape, fan_in):
        return jax.random.normal(k, shape, f32) * (fan_in ** -0.5)

    x = jax.random.normal(ks[0], (BATCH, SEQ, D_MODEL), f32)
    norm_pre = 1.0 + 0.05 * jax.random.normal(ks[1], (DEPTH, D_MODEL), f32)
    norm_post = 1.0 + 0.05 * jax.random.normal(ks[2], (DEPTH, D_MODEL), f32)
    lru_w_in = nrm(ks[3], (N_LRU, D_MODEL, 2 * D_RNN), D_MODEL)
    lru_conv_w = nrm(ks[4], (N_LRU, CONV_W, D_RNN), CONV_W)
    lru_conv_b = 0.02 * jax.random.normal(ks[5], (N_LRU, D_RNN), f32)
    lru_w_a = nrm(ks[6], (N_LRU, N_GATE_BLOCKS, BLOCK_W, BLOCK_W), BLOCK_W)
    lru_b_a = 0.02 * jax.random.normal(ks[7], (N_LRU, D_RNN), f32)
    lru_w_x = nrm(ks[8], (N_LRU, N_GATE_BLOCKS, BLOCK_W, BLOCK_W), BLOCK_W)
    lru_b_x = 0.02 * jax.random.normal(ks[9], (N_LRU, D_RNN), f32)
    a_c = jax.random.uniform(ks[10], (N_LRU, D_RNN), f32, minval=0.9, maxval=0.999)
    sig = a_c ** (1.0 / C_RG)
    lru_lambda = jnp.log(sig) - jnp.log1p(-sig)
    lru_w_out = nrm(ks[11], (N_LRU, D_RNN, D_MODEL), D_RNN)
    ret_w_in = nrm(ks[12], (N_RET, D_MODEL, 2 * QK_DIM + 2 * V_DIM), D_MODEL)
    ret_w_out = nrm(ks[13], (N_RET, V_DIM, D_MODEL), V_DIM)
    return {"x": x, "norm_pre": norm_pre, "norm_post": norm_post,
            "lru_w_in": lru_w_in, "lru_conv_w": lru_conv_w, "lru_conv_b": lru_conv_b,
            "lru_w_a": lru_w_a, "lru_b_a": lru_b_a, "lru_w_x": lru_w_x, "lru_b_x": lru_b_x,
            "lru_lambda": lru_lambda, "lru_w_out": lru_w_out,
            "ret_w_in": ret_w_in, "ret_w_out": ret_w_out}

def second_block(x, norm_pre, norm_post, lru_w_in, lru_conv_w, lru_conv_b, lru_w_a, lru_b_a,
              lru_w_x, lru_b_x, lru_lambda, lru_w_out, ret_w_in, ret_w_out):
    s = x.shape[1]
    pos = jnp.arange(s, dtype=jnp.float32)
    inv_freq = ROPE_BASE ** (-jnp.arange(0, QK_HEAD, 2, dtype=jnp.float32) / QK_HEAD)
    ang = pos[:, None] * inv_freq[None, :]
    cos, sin = jnp.cos(ang), jnp.sin(ang)
    for layer in range(DEPTH):
        h = rms_norm(x, norm_pre[layer])
        j = layer // N_MIXERS
        if layer % N_MIXERS == 0:
            o = rglru_mixer(h, lru_w_in[j], lru_conv_w[j], lru_conv_b[j], lru_w_a[j], lru_b_a[j],
                            lru_w_x[j], lru_b_x[j], lru_lambda[j], lru_w_out[j])
        else:
            o = retention_mixer(h, ret_w_in[j], ret_w_out[j], cos, sin)
        x = x + rms_norm(o, norm_post[layer])
    return x


def setup_inputs(seed=0):
    out = dict(first_inputs(seed))
    for name, value in second_inputs(seed + 1).items():
        if name != "x":
            out[name + "_2"] = value
    return out


def reference(
    x, a_norm, a_w_in, a_w_out, b_norm, b_w_in, b_f, b_w_out, ffn_norm, ffn_w_gu, ffn_w_down,
    final_norm, norm_pre_2, norm_post_2, lru_w_in_2, lru_conv_w_2, lru_conv_b_2, lru_w_a_2,
    lru_b_a_2, lru_w_x_2, lru_b_x_2, lru_lambda_2, lru_w_out_2, ret_w_in_2, ret_w_out_2,
):
    x = first_block(
        x, a_norm, a_w_in, a_w_out, b_norm, b_w_in, b_f, b_w_out, ffn_norm, ffn_w_gu,
        ffn_w_down, final_norm,
    )
    return second_block(
        x, norm_pre_2, norm_post_2, lru_w_in_2, lru_conv_w_2, lru_conv_b_2, lru_w_a_2,
        lru_b_a_2, lru_w_x_2, lru_b_x_2, lru_lambda_2, lru_w_out_2, ret_w_in_2, ret_w_out_2,
    )


_drawn_inputs = setup_inputs


def setup_inputs(seed=0):
    import zlib

    import numpy as np

    out = dict(_drawn_inputs(seed))
    spreads = {}
    factors = {'a_norm': 3.685, 'b_norm': 3.298, 'lru_b_a_2': 8.0, 'lru_b_x_2': 7.492}
    for name, (base, spread) in spreads.items():
        noise = np.random.default_rng([zlib.crc32(name.encode()), seed]).standard_normal(out[name].shape)
        drawn = base * np.exp(spread * noise) if base else spread * noise
        out[name] = __import__('jax').numpy.asarray(drawn.astype(out[name].dtype))
    for name, factor in factors.items():
        out[name] = (out[name] * factor).astype(out[name].dtype)
    return out
```

```python
from contextlib import ExitStack

import numpy as np
import concourse.bass as bass
from concourse import mybir

F32 = mybir.dt.float32
F32R = mybir.dt.float32r
ALU = mybir.AluOpType
ACT = mybir.ActivationFunctionType
AX = mybir.AxisListType

P = 128
T = 512
TB = T // P
D = 1024
DT = D // P
NH = 16
HD = 64
FT = 22
LT = 12
RH = 4
RMS_EPS = 1e-6
GN_EPS = 1e-5
MASKED = -1e30
RING = 4
UNIT = 8 * P

PHASES = [("A", 72), ("AO", 8), ("F0", 44), ("D0", 22), ("BF", 1), ("B", 24), ("BO", 8), ("F1", 44),
          ("D1", 22), ("L", 24), ("LG", 8), ("LO", 12), ("R", 48), ("RO", 16)]
START = {}
_n = 0
for _name, _count in PHASES:
    START[_name] = _n
    _n += _count
UNITS = _n

VEC = {}
_n = 0
for _name, _count in [("a_norm", 8), ("ffn0", 8), ("b_norm", 8), ("ffn1", 8), ("final", 8), ("pre0", 8),
                      ("post0", 8), ("pre1", 8), ("conv0", LT), ("conv1", LT), ("conv2", LT), ("conv3", LT),
                      ("conv_b", LT), ("b_a", LT), ("b_x", LT), ("lam", LT), ("b_f", 1)]:
    VEC[_name] = _n
    _n += _count
NVEC = _n
IDENT, ONES, BAND, CLASS, NCST = 0, 128, 256, 512, 640
GATE_BLOCKS = [(0, 0), (1, 0), (0, 1), (1, 1), (2, 1), (1, 2), (2, 2)]


def program(nc, ws, x, vec, cst, sel, turn_a, turn_r, decay, post1, out):
    with ExitStack() as ctx:
        def sem(name):
            return ctx.enter_context(nc.semaphore(name))

        top = [nc.sbuf_base + (-nc.sbuf_base) % 32]

        def sb(name, shape, dt=F32, at=None):
            size = int(np.prod(shape[1:])) * 4
            where = top[0] if at is None else at
            t = nc.alloc_sbuf_tensor_at(name, shape, dt, offset=where)
            if at is None:
                top[0] += size + (-size) % 32
            return t

        R = sb("R", [P, DT, T])
        XH = sb("XH", [P, DT, T], F32R)
        XL = sb("XL", [P, DT, T], F32R)
        WR = sb("WR", [P, RING, UNIT])
        WH = sb("WH", [P, RING, UNIT], F32R)
        WL = sb("WL", [P, RING, UNIT], F32R)
        VC = sb("VC", [P, NVEC])
        CST = sb("CST", [P, NCST])
        RB = sb("RB", [P, T + 16])
        squares_at = top[0]
        SQT = sb("SQT", [P, T])
        SQS = sb("SQS", [P, T])
        arena = top[0]
        limit = nc.sbuf_usable_end

        class Arena:
            def __init__(self):
                self.at = arena

            def __call__(self, name, shape, dt=F32):
                t = sb(name, shape, dt, at=self.at)
                size = int(np.prod(shape[1:])) * 4
                self.at += size + (-size) % 32
                assert self.at <= limit, (name, self.at - limit)
                return t

        a = Arena()
        A_Q = a("A_Q", [P, 4, T])
        A_K = a("A_K", [P, 4, T])
        A_V = a("A_V", [P, TB, T])
        A_O = a("A_O", [P, 3, DT, T])
        A_COS = a("A_COS", [P, T])
        A_SIN = a("A_SIN", [P, T])
        A_P = a("A_P", [P, 3, T])
        A_PT = a("A_PT", [P, 2, T])
        A_T1 = a("A_T1", [P, 2, T])
        A_SH = a("A_SH", [P, 2, T])
        A_MX = a("A_MX", [P, 3, NH, TB])
        A_NM = a("A_NM", [P, 3, NH, TB])
        A_DEN = a("A_DEN", [P, 3, NH, TB])
        A_SEL = a("A_SEL", [NH, D])
        XTOK = sb("XTOK", [P, TB, D], at=arena)
        a = Arena()
        A_MN = a("A_MN", [NH, 3, T])
        A_DN = a("A_DN", [NH, 3, T])
        A_M = a("A_M", [NH, T])
        A_Z = a("A_Z", [NH, T])
        A_Y = a("A_Y", [P, 2, T])
        A_U = sb("A_U", [P, 3, T], at=arena + 3 * 8192 + 3 * 16384 + 4096)
        a = Arena()
        HH = a("HH", [P, FT, T], F32R)
        HL = a("HL", [P, FT, T], F32R)
        F_G = a("F_G", [P, 2, T])
        F_U = a("F_U", [P, 2, T])
        F_S = a("F_S", [P, 2, T])
        a = Arena()
        B_Q = a("B_Q", [P, 4, T])
        B_K = a("B_K", [P, 4, T])
        B_V = a("B_V", [P, TB, T])
        B_O = a("B_O", [P, DT, T])
        B_CB = a("B_CB", [P, 2, T])
        B_DG = a("B_DG", [P, 2, T])
        B_P = a("B_P", [P, 3, T])
        B_PT = a("B_PT", [P, 2, T])
        B_MX = a("B_MX", [P, NH, TB, 2])
        B_NM = a("B_NM", [P, NH, TB])
        B_DEN = a("B_DEN", [P, NH, TB])
        B_SEL = a("B_SEL", [NH, D])
        B_RD = a("B_RD", [NH, T])
        B_NC = a("B_NC", [NH, T])
        B_Z = a("B_Z", [NH, T])
        B_E = a("B_E", [NH, T])
        B_S = a("B_S", [NH, T])
        B_W = a("B_W", [NH, T])
        B_A = a("B_A", [NH, T])
        B_1 = a("B_1", [NH, T])
        a = Arena()
        CH = a("CH", [P, LT, T], F32R)
        CL = a("CL", [P, LT, T], F32R)
        L_G = a("L_G", [P, LT, T])
        L_R = a("L_R", [P, 3, T])
        L_I = a("L_I", [P, 3, T])
        L_A = a("L_A", [P, 3, T])
        L_E = a("L_E", [P, 3, T])
        L_X = a("L_X", [P, 3, T])
        L_S = a("L_S", [P, 8, LT])
        tmp = arena + 4 * LT * T * 3
        L_XR = sb("L_XR", [P, 2, T + 3 + 1], at=tmp)
        L_XC = sb("L_XC", [P, 2, T], at=tmp + 4160)
        L_SG = sb("L_SG", [P, 2, T], at=tmp + 4160 + 4096)
        L_O = sb("L_O", [P, DT, T], at=tmp)
        a = Arena()
        YH = a("YH", [P, 16, T], F32R)
        YL = a("YL", [P, 16, T], F32R)
        R_QK = a("R_QK", [P, 4, T])
        R_V = a("R_V", [P, TB, T])
        R_G = a("R_G", [P, TB, T])
        R_PT = a("R_PT", [P, 1280])
        R_D = a("R_D", [P, T])
        R_COS = a("R_COS", [P, T])
        R_SIN = a("R_SIN", [P, T])
        R_SG = sb("R_SG", [P, 2, T], at=squares_at)
        R_ST = a("R_ST", [P, 64])
        base_qk = arena + 2 * 16 * T * 4
        OUT = sb("OUT", [P, TB, D], at=base_qk)
        GAIN = sb("GAIN", [P, D], at=base_qk + 16384)
        R_T = [sb("R_T1", [P, 2, T], at=base_qk + 16384), sb("R_T2", [P, 2, T], at=base_qk + 16384 + 4096)]

        PS = ctx.enter_context(nc.psum_tensor("PS", [P, 8, 512], F32))

        ident = CST[:, IDENT:IDENT + P]
        ones = CST[:, ONES:ONES + P]

        landed = [sem(f"landed{i}") for i in range(RING)]
        hi_ready = sem("hi_ready")
        lo_ready = sem("lo_ready")
        unit_used = sem("unit_used")
        consts_in, x_in, rota_in, rotr_in, gain_in, decay_in, sel_in = (
            sem("consts_in"), sem("x_in"), sem("rota_in"), sem("rotr_in"), sem("gain_in"), sem("decay_in"),
            sem("sel_in"))
        x_turned = sem("x_turned")
        r_done = sem("r_done")
        x_hi, x_lo = sem("x_hi"), sem("x_lo")
        sq_mul, sq_sum = sem("sq_mul"), sem("sq_sum")
        stat_done, rb_var, rb_std, rb_ready = sem("stat_done"), sem("rb_var"), sem("rb_std"), sem("rb_ready")
        tab_ready = sem("tab_ready")
        rot_a, rot_sh, rot_m, qk_ready, v_ready = (
            sem("rot_a"), sem("rot_sh"), sem("rot_m"), sem("qk_ready"), sem("v_ready"))
        s_done, max_done, nm_ready, p_ready = sem("s_done"), sem("max_done"), sem("nm_ready"), sem("p_ready")
        t_done, pt_copied, pv_done, o_copied = sem("t_done"), sem("pt_copied"), sem("pv_done"), sem("o_copied")
        st_turned, st_copied, st_step, st_exp, st_z = (
            sem("st_turned"), sem("st_copied"), sem("st_step"), sem("st_exp"), sem("st_z"))
        bc_done, bc_used, y_sum = sem("bc_done"), sem("bc_used"), sem("y_sum")
        g_ready, u_ready, sg_ready, gs_ready, ht_ready, hh_ready, hl_ready = (
            sem("g_ready"), sem("u_ready"), sem("sg_ready"), sem("gs_ready"), sem("ht_ready"), sem("hh_ready"),
            sem("hl_ready"))
        fz_done, lf_step, lf_exp, nc_ready, cb_done, cb_ready, dg_ready = (
            sem("fz_done"), sem("lf_step"), sem("lf_exp"), sem("nc_ready"), sem("cb_done"), sem("cb_ready"),
            sem("dg_ready"))
        bq_ready = sem("bq_ready")
        xr_ready, xc_ready, conv_step, ch_ready, cl_ready = (
            sem("xr_ready"), sem("xc_ready"), sem("conv_step"), sem("ch_ready"), sem("cl_ready"))
        lg_ready, lsg_ready, lgs_ready = sem("lg_ready"), sem("lsg_ready"), sem("lgs_ready")
        ls_step, ls_exp, ls_ready = sem("ls_step"), sem("ls_exp"), sem("ls_ready")
        sig_done, ae_done, q_done, sqrt_done, xs_done, ix_done, bt_done, h_done, y_done = (
            sem("sig_done"), sem("ae_done"), sem("q_done"), sem("sqrt_done"), sem("xs_done"), sem("ix_done"),
            sem("bt_done"), sem("h_done"), sem("y_done"))
        lo_copied, post_mul = sem("lo_copied"), sem("post_mul")
        rt_turned, rt_ready = sem("rt_turned"), sem("rt_ready")
        rr_step, rr_ready, rv_ready, rg_ready, rsg_ready, rgs_ready = (
            sem("rr_step"), sem("rr_ready"), sem("rv_ready"), sem("rg_ready"), sem("rsg_ready"), sem("rgs_ready"))
        rs_done, rpt_ready, ro_done, gn_step, gn_std, gn_ready, rn_ready, ry_ready, yt_done, yh_ready, yl_ready = (
            sem("rs_done"), sem("rpt_ready"), sem("ro_done"), sem("gn_step"), sem("gn_std"), sem("gn_ready"),
            sem("rn_ready"), sem("ry_ready"), sem("yt_done"), sem("yh_ready"), sem("yl_ready"))
        ss_done, fin_step, fin_std, o_scaled, o_ready, out_done = (
            sem("ss_done"), sem("fin_step"), sem("fin_std"), sem("o_scaled"), sem("o_ready"), sem("out_done"))

        CLASSES = [1, 4, 4]

        def token_block(ap, g, b):
            c = CLASSES[g]
            if c == 1:
                return ap[:, b * P:(b + 1) * P]
            v = ap.rearrange("p (l c) -> p c l", c=c)
            return v[:, b, :]

        def by_class(ap, g):
            return ap.rearrange("p (l c) -> p c l", c=CLASSES[g])

        def classes_of(ap, g):
            return ap.rearrange("p (c l) -> p c l", c=CLASSES[g])

        def by_step(ap, g):
            return ap.rearrange("p (c l) -> p l c", c=CLASSES[g])

        def steps_of(ap, g):
            return ap.rearrange("p (l c) -> p l c", c=CLASSES[g])

        def dilated_items(g):
            if g == 0:
                segs = [[(0, [0], 0), (1, [0, 1], P)], [(2, [1, 2], 0), (3, [2, 3], 2 * P)]]
            else:
                segs = [[(b, [b], b * P) for b in range(TB)]]
            return [(h, s) for h in range(8) for s in segs]

        FORGET_ITEMS = [(h, [(b, list(range(b + 1)), 0)]) for h in range(8) for b in range(TB)]
        ITEMS_A = [dilated_items(g) for g in range(3)]
        BODIES = [(g, half) for g in range(3) for half in range(2)]
        ITEM0, SEG0 = [], []
        n = m = 0
        for g, half in BODIES:
            ITEM0.append(n)
            SEG0.append(m)
            n += len(ITEMS_A[g])
            m += sum(len(s) for _, s in ITEMS_A[g])
        for half in range(2):
            ITEM0.append(n)
            n += len(FORGET_ITEMS)
        ITEM0.append(n)

        def width(segs):
            return segs[-1][2] + P * len(segs[-1][1])

        def rstd_col(g, b):
            return RB[:, T + 4 * g + b:T + 4 * g + b + 1]

        U = START
        PT0 = [0, 512, 896, 1152]
        R_TF = sb("R_TF", [P, 2, T], at=base_qk + 16384 + 4096)
        rr_bn, gn_r = sem("rr_bn"), sem("gn_r")

        block = ctx.enter_context(nc.Block())

        @block.sync
        def _(sp):
            sp.dma_start(XTOK[:, :, :], x.rearrange("(b p) d -> p b d", p=P)).then_inc(x_in, 16)
            sp.dma_start(CST[:, :], cst).then_inc(consts_in, 16)
            sp.dma_start(VC[:, :], vec).then_inc(consts_in, 16)
            for u in range(UNITS):
                if u >= RING:
                    sp.wait_ge(hi_ready, u - RING + 1)
                    sp.wait_ge(lo_ready, u - RING + 1)
                sp.dma_start(WR[:, u % RING, :], ws[u]).then_inc(landed[u % RING], 16)
            for tb in range(TB):
                sp.wait_ge(o_ready, tb + 1)
                sp.dma_start(out[tb * P:(tb + 1) * P, :], OUT[:, tb, :]).then_inc(out_done, 16)
            sp.wait_ge(out_done, 16 * TB)

        @block.tensor
        def _(pe):
            def unit(u, kpair, hi, lo, bank, first, last, stationary, ready=None):
                s = u % RING
                pe.wait_ge(lo_ready, u + 1)
                for kk in range(2):
                    k = 2 * kpair + kk
                    if ready is not None:
                        ready(k)
                    for o in range(4):
                        if stationary:
                            cols = slice(kk * T + o * P, kk * T + (o + 1) * P)
                            pairs = [(WH[:, s, cols], hi[:, k, :]), (WH[:, s, cols], lo[:, k, :]),
                                     (WL[:, s, cols], hi[:, k, :])]
                        else:
                            cols = slice(kk * T, (kk + 1) * T)
                            xh, xl = stationary_x(hi, k, o), stationary_x(lo, k, o)
                            pairs = [(xh, WH[:, s, cols]), (xh, WL[:, s, cols]), (xl, WH[:, s, cols])]
                        for i, (l, r) in enumerate(pairs):
                            mm = pe.matmul(PS[:, bank + o, :], l, r, start=first and kk == 0 and i == 0,
                                           stop=last and kk == 1 and i == 2)
                mm.then_inc(unit_used, 1)

            order = [0]

            def stationary_x(t, k, o):
                return token_block(t[:, k, :], order[0], o)

            def group(u, kpairs, hi, lo, bank, stationary=True, ready=None):
                for j in range(kpairs):
                    unit(u + j, j, hi, lo, bank, j == 0, j == kpairs - 1, stationary, ready)

            def statistics(s, bank, groups=()):
                pe.wait_ge(sq_sum, 7 * (s + 1))
                mm = pe.matmul(PS[:, bank, :], ones, SQS[:, :], start=True, stop=True)
                for g in groups:
                    for b in range(TB):
                        mm = pe.matmul(PS[:, bank + 1, 4 * g + b:4 * g + b + 1], token_block(SQS[:, :], g, b),
                                       ones[:, 0:1], start=True, stop=True)
                mm.then_inc(stat_done, 1)

            def x_ready(v):
                def wait(k):
                    pe.wait_ge(x_hi, 8 * v + k + 1)
                    pe.wait_ge(x_lo, 8 * v + k + 1)
                return wait

            def attention(items, item0, Q, K, V, PR, PT, forget=None):
                N = len(items)
                for n in range(N + 3):
                    if n < N:
                        h, segs = items[n]
                        rows = slice(HD * (h % 2), HD * (h % 2) + HD)
                        if n >= 2:
                            pe.wait_ge(max_done, item0 + n - 1)
                        if forget is not None and n % TB == 0:
                            forget(h)
                        for qb, kbs, c in segs:
                            mm = pe.matmul(PS[:, 4 + n % 2, c:c + P * len(kbs)],
                                           Q[rows, h // 2, qb * P:(qb + 1) * P],
                                           K[rows, h // 2, kbs[0] * P:(kbs[-1] + 1) * P], start=True, stop=True)
                        mm.then_inc(s_done, 1)
                    m = n - 2
                    if 0 <= m < N:
                        h, segs = items[m]
                        pe.wait_ge(p_ready, item0 + m + 1)
                        if m >= 2:
                            pe.wait_ge(pt_copied, item0 + m - 1)
                        for c in range(0, width(segs), P):
                            mm = pe.transpose(PS[:, 6 + m % 2, c:c + P], PR[:, m % 3, c:c + P], ident)
                        mm.then_inc(t_done, 1)
                    m = n - 3
                    if 0 <= m < N:
                        h, segs = items[m]
                        rows = slice(HD * (h % 2), HD * (h % 2) + HD)
                        pe.wait_ge(pt_copied, item0 + m + 1)
                        pair = h // 2
                        if pair >= 2 and h % 2 == 0:
                            pe.wait_ge(o_copied, PAIR0[0] + pair - 1)
                        for qb, kbs, c in segs:
                            for j, kb in enumerate(kbs):
                                mm = pe.matmul(PS[rows, pair % 2, qb * P:(qb + 1) * P],
                                               V[:, kb, h * HD:(h + 1) * HD],
                                               PT[:, m % 2, c + j * P:c + (j + 1) * P],
                                               start=j == 0, stop=j == len(kbs) - 1)
                        mm.then_inc(pv_done, 1)

            PAIR0 = [0]

            pe.wait_ge(x_in, 16)
            pe.wait_ge(consts_in, 32)
            for k in range(DT):
                for b in range(TB):
                    mm = pe.transpose(PS[:, k, b * P:(b + 1) * P], XTOK[:, b, k * P:(k + 1) * P], ident)
                mm.then_inc(x_turned, 1)

            pe.wait_ge(r_done, 8)
            statistics(0, 6, (0, 1, 2))
            for m, (g, half) in enumerate(BODIES):
                u = U["A"] + 12 * m
                if m:
                    pe.wait_ge(o_copied, 4 * m)
                order[0] = g
                group(u, 4, XH, XL, 0, ready=x_ready(0))
                pe.wait_ge(rb_var, 1)
                group(u + 4, 4, XH, XL, 4)
                pe.wait_ge(rot_sh, 8 * m + 4)
                group(u + 8, 4, XH, XL, 0, stationary=False)
                order[0] = 0
                pe.wait_ge(rot_sh, 8 * m + 8)
                pe.wait_ge(qk_ready, 8 * m + 8)
                pe.wait_ge(v_ready, 4 * m + 4)
                PAIR0[0] = 4 * m
                attention(ITEMS_A[g], ITEM0[m], A_Q, A_K, A_V, A_P, A_PT)
            pe.wait_ge(o_copied, 24)
            for g in range(3):
                for b in range(TB):
                    pe.transpose(PS[0:NH, g, b * P:(b + 1) * P], A_NM[:, g, :, b], ident)
                    mm = pe.transpose(PS[0:NH, 3 + g, b * P:(b + 1) * P], A_DEN[:, g, :, b], ident)
            mm.then_inc(st_turned, 1)
            pe.wait_ge(st_z, 1)
            pe.wait_ge(sel_in, 16)
            for t in range(DT):
                for g in range(3):
                    n = 3 * t + g
                    if n >= 8:
                        pe.wait_ge(bc_used, n - 7)
                    pe.matmul(PS[:, n % 8, :], A_SEL[:, t * P:(t + 1) * P], A_MN[:, g, :], start=True, stop=True).then_inc(bc_done, 1)
            pe.wait_ge(bc_used, 24)
            for d in range(2):
                group(U["AO"] + 4 * d, 4, XH, XL, 4 * d, ready=x_ready(1))

            def swiglu(layer, v, s):
                f, dn = U[f"F{layer}"], U[f"D{layer}"]
                statistics(s, 0)
                for j in range(11):
                    n = 11 * layer + j
                    if j == 1:
                        pe.wait_ge(rb_var, s + 1)
                    if j >= 2:
                        pe.wait_ge(u_ready, n - 1)
                    group(f + 4 * j, 4, XH, XL, 4 if j % 2 == 0 else 0, ready=x_ready(v))
                pe.wait_ge(u_ready, 11 * layer + 10)

                def hidden(k):
                    pe.wait_ge(hh_ready, 11 * layer + k // 2 + 1)
                    pe.wait_ge(hl_ready, 11 * layer + k // 2 + 1)
                for d in range(2):
                    if d:
                        pe.wait_ge(u_ready, 11 * layer + 11)
                    group(dn + 11 * d, 11, HH, HL, 4 * d, ready=hidden)

            swiglu(0, 2, 1)

            statistics(2, 6, (0,))
            u = U["BF"]
            pe.wait_ge(lo_ready, u + 1)
            for k in range(DT):
                x_ready(3)(k)
                cols = slice(k * P, (k + 1) * P)
                pe.matmul(PS[:, 5, :], WH[:, u % RING, cols], XH[:, k, :], start=k == 0, stop=False)
                pe.matmul(PS[:, 5, :], WH[:, u % RING, cols], XL[:, k, :], start=False, stop=False)
                mm = pe.matmul(PS[:, 5, :], WL[:, u % RING, cols], XH[:, k, :], start=False, stop=k == DT - 1)
            mm.then_inc(unit_used, 1)

            def broadcast_gate(half):
                def run(h):
                    n = 8 * half + h
                    if n:
                        pe.wait_ge(cb_ready, n)
                    pe.matmul(PS[:, 2, :], ident[0:NH, n:n + 1].to_broadcast([NH, P]), B_NC[:, :],
                              start=True, stop=True).then_inc(cb_done, 1)
                return run
            for half in range(2):
                u = U["B"] + 12 * half
                if half:
                    pe.wait_ge(o_copied, 28)
                    pe.wait_ge(cb_ready, 8)
                group(u, 4, XH, XL, 0)
                pe.wait_ge(rb_var, 3)
                pe.wait_ge(lf_step, 1)
                group(u + 4, 4, XH, XL, 4)
                pe.wait_ge(bq_ready, 8 * half + 4)
                group(u + 8, 4, XH, XL, 0, stationary=False)
                pe.wait_ge(bq_ready, 8 * half + 8)
                pe.wait_ge(v_ready, 24 + 4 * half + 4)
                pe.wait_ge(nc_ready, 1)
                PAIR0[0] = 24 + 4 * half
                attention(FORGET_ITEMS, ITEM0[6 + half], B_Q, B_K, B_V, B_P, B_PT, broadcast_gate(half))
            pe.wait_ge(o_copied, 32)
            pe.wait_ge(st_step, 8)
            for b in range(TB):
                mm = pe.transpose(PS[0:NH, 0, b * P:(b + 1) * P], B_DEN[:, :, b], ident)
            mm.then_inc(st_turned, 1)
            pe.wait_ge(st_z, 2)
            pe.wait_ge(sel_in, 32)
            for t in range(DT):
                if t >= 4:
                    pe.wait_ge(bc_used, 24 + t - 3)
                pe.matmul(PS[:, 4 + t % 4, :], B_SEL[:, t * P:(t + 1) * P], B_RD[:, :], start=True, stop=True).then_inc(bc_done, 1)
            for d in range(2):
                if d:
                    pe.wait_ge(bc_used, 32)
                group(U["BO"] + 4 * d, 4, XH, XL, 4 * d, ready=x_ready(4))
            swiglu(1, 5, 3)
            statistics(4, 6)

            statistics(5, 6)
            for j in range(3):
                if j:
                    pe.wait_ge(xr_ready, 4 * j)
                group(U["L"] + 8 * j, 4, XH, XL, 0, ready=x_ready(6))
                pe.wait_ge(rb_var, 6)
                if j:
                    pe.wait_ge(lg_ready, 4 * j)
                group(U["L"] + 8 * j + 4, 4, XH, XL, 4)
            pe.wait_ge(xr_ready, 12)
            pe.wait_ge(lg_ready, 12)
            for j in range(4):
                pe.wait_ge(ch_ready, 3 * j + 3)
                pe.wait_ge(cl_ready, 3 * j + 3)
                for which in range(2):
                    u = U["LG"] + 2 * j + which
                    s = u % RING
                    pe.wait_ge(lo_ready, u + 1)
                    if j:
                        pe.wait_ge(sig_done, 6 * (j - 1) + 3 * which + 3)
                    for o in range(3):
                        blocks = [(n, i) for n, (i, oo) in enumerate(GATE_BLOCKS) if oo == o]
                        for n, i in blocks:
                            cols = slice(n * P, (n + 1) * P)
                            b = PS[:, 4 * which + o, :]
                            pe.matmul(b, WH[:, s, cols], CH[:, 3 * j + i, :], start=n == blocks[0][0], stop=False)
                            pe.matmul(b, WH[:, s, cols], CL[:, 3 * j + i, :], start=False, stop=False)
                            mm = pe.matmul(b, WL[:, s, cols], CH[:, 3 * j + i, :], start=False,
                                           stop=n == blocks[-1][0])
                    mm.then_inc(unit_used, 1)
            pe.wait_ge(sig_done, 24)

            def recurrent(k):
                pe.wait_ge(ch_ready, LT + k + 1)
                pe.wait_ge(cl_ready, LT + k + 1)
            for d in range(2):
                group(U["LO"] + 6 * d, 6, CH, CL, 4 * d, ready=recurrent)
            statistics(6, 6)

            statistics(7, 6, (0,))
            for h in range(RH):
                u = U["R"] + 12 * h
                if h:
                    pe.wait_ge(rn_ready, 4 * h)
                group(u, 4, XH, XL, 0, ready=x_ready(7))
                pe.wait_ge(rb_var, 8)
                if h:
                    pe.wait_ge(yl_ready, 4 * h)
                    pe.wait_ge(yh_ready, 4 * h)
                group(u + 4, 4, XH, XL, 4, stationary=False)
                pe.wait_ge(rr_step, 4 * h + 4)
                group(u + 8, 4, XH, XL, 0, stationary=False)
                pe.wait_ge(rr_ready, 4 * h + 4)
                pe.wait_ge(rv_ready, 4 * h + 4)
                for kb in range(TB):
                    for c in range(2):
                        mm = pe.matmul(PS[:, 4 + kb, 0:T - kb * P], R_QK[:, 2 + c, kb * P:(kb + 1) * P],
                                       R_QK[:, c, kb * P:T], start=c == 0, stop=c == 1)
                    mm.then_inc(rs_done, 1)
                pe.wait_ge(rsg_ready, 4 * h + 4)
                pe.wait_ge(rg_ready, 4 * h + 4)
                for qb in range(TB):
                    pe.wait_ge(rpt_ready, 4 * h + qb + 1)
                    for kb in range(qb + 1):
                        mm = pe.matmul(PS[:, qb, :], R_PT[:, PT0[kb] + (qb - kb) * P:PT0[kb] + (qb - kb + 1) * P],
                                       R_V[:, kb, :], start=kb == 0, stop=kb == qb)
                    mm.then_inc(ro_done, 1)
                pe.wait_ge(ry_ready, 4 * h + 4)
                for j in range(4):
                    for b in range(TB):
                        mm = pe.transpose(PS[:, 4 + j, b * P:(b + 1) * P], R_G[:, b, j * P:(j + 1) * P], ident)
                    mm.then_inc(yt_done, 1)
            pe.wait_ge(rn_ready, 16)
            for b in range(TB):
                for k in range(DT):
                    mm = pe.transpose(PS[:, 2 * (b % 2) + k // 4, (k % 4) * P:(k % 4 + 1) * P],
                                      R[:, k, b * P:(b + 1) * P], ident)
                mm.then_inc(rt_turned, 1)
                if b in (1, 2):
                    pe.wait_ge(rt_ready, b)
            pe.wait_ge(rt_ready, 4)
            pe.wait_ge(yl_ready, 16)
            pe.wait_ge(yh_ready, 16)
            for d in range(2):
                group(U["RO"] + 8 * d, 8, YH, YL, 4 * d, stationary=False)

        @block.scalar
        def _(act):
            def split(a, b):
                for u in range(a, min(b, UNITS)):
                    s = u % RING
                    act.wait_ge(landed[s], 16 * (u // RING + 1))
                    if u >= RING:
                        act.wait_ge(unit_used, u - RING + 1)
                    nc.scalar.activation(WH[:, s, :], WR[:, s, :], ACT.Copy).then_inc(hi_ready, 1)

            def build_x(v, version, gain, before, ks=range(DT)):
                for k in ks:
                    act.wait_ge(r_done, 8 * version + k + 1)
                    if k == 0:
                        act.wait_ge(unit_used, before)
                    nc.scalar.activation(XH[:, k, :], R[:, k, :], ACT.Copy,
                                         scale=VC[:, VEC[gain] + k:VEC[gain] + k + 1]).then_inc(x_hi, 1)

            def root(s, width=T):
                act.wait_ge(rb_var, s + 1)
                nc.scalar.activation(RB[:, 0:width], RB[:, 0:width], ACT.Sqrt).then_inc(rb_std, 1)

            def exps(items, item0, PR, NM, DEN):
                for n, (h, segs) in enumerate(items):
                    act.wait_ge(nm_ready, item0 + n + 1)
                    for qb, kbs, c in segs:
                        w = slice(c, c + P * len(kbs))
                        e = nc.scalar.activation(PR[:, n % 3, w], PR[:, n % 3, w], ACT.Exp, bias=NM(h, qb),
                                                 accum_out=DEN(h, qb))
                    e.then_inc(p_ready, 1)

            act.dma_start(A_COS[:, :], turn_a[0]).then_inc(rota_in, 16)
            act.dma_start(A_SIN[:, :], turn_a[1]).then_inc(rota_in, 16)
            act.dma_start(A_SEL[:, :], sel).then_inc(sel_in, 16)
            split(0, 4)
            act.wait_ge(consts_in, 32)
            build_x(0, 0, "a_norm", 0)
            root(0, T + 12)
            for m, (g, half) in enumerate(BODIES):
                u = U["A"] + 12 * m
                split(u + 4, u + 16)
                act.wait_ge(unit_used, u + 12)
                act.wait_ge(rb_ready, 1)
                if m:
                    act.wait_ge(pv_done, ITEM0[m])
                for b in range(TB):
                    nc.scalar.activation(A_V[:, b, :], PS[:, b, :], ACT.Copy, scale=rstd_col(g, b))\
                        .then_inc(v_ready, 1)
                exps(ITEMS_A[g], ITEM0[m], A_P, lambda h, b: A_NM[:, g, 8 * half + h, b:b + 1],
                     lambda h, b: A_DEN[:, g, 8 * half + h, b:b + 1])
            act.wait_ge(st_step, 5)
            nc.scalar.activation(A_MN[:, :, :], A_MN[:, :, :], ACT.Exp).then_inc(st_exp, 1)
            for t in range(DT):
                act.wait_ge(y_sum, 2 * t + 2)
                nc.scalar.activation(XH[:, t, :], A_Y[:, t % 2, :], ACT.Copy).then_inc(x_hi, 1)
            split(U["AO"] + 4, U["AO"] + 8)

            def swiglu(layer, v, version, s, gain):
                f, dn = U[f"F{layer}"], U[f"D{layer}"]
                split(f, f + 4)
                build_x(v, version, gain, f)
                root(s)
                for j in range(11):
                    n = 11 * layer + j
                    split(f + 4 * j + 4, f + 4 * j + 8)
                    act.wait_ge(g_ready, n + 1)
                    if j:
                        act.wait_ge(gs_ready, n)
                    nc.scalar.activation(F_S[:, :, :], F_G[:, :, :], ACT.Sigmoid).then_inc(sg_ready, 1)
                    act.wait_ge(ht_ready, n + 1)
                    nc.scalar.activation(HH[:, 2 * j:2 * j + 2, :], F_U[:, :, :], ACT.Copy).then_inc(hh_ready, 1)
                split(dn + 4, dn + 15)

            swiglu(0, 2, 1, 1, "ffn0")

            d0 = U["D0"]
            build_x(3, 2, "b_norm", d0, range(0, 4))
            split(d0 + 15, d0 + 26)
            build_x(3, 2, "b_norm", d0, range(4, 8))
            root(2, T + 4)
            act.dma_start(B_SEL[:, :], sel).then_inc(sel_in, 16)
            split(U["BF"] + 4, U["BF"] + 5)
            act.wait_ge(lf_step, 3)
            nc.scalar.activation(B_E[:, :], B_A[:, :], ACT.Exp, scale=-1.0).then_inc(lf_exp, 1)
            for half in range(2):
                u = U["B"] + 12 * half
                split(u + 4, u + 16)
                act.wait_ge(unit_used, u + 12)
                act.wait_ge(rb_ready, 3)
                if half:
                    act.wait_ge(pv_done, ITEM0[7])
                for b in range(TB):
                    nc.scalar.activation(B_V[:, b, :], PS[:, b, :], ACT.Copy, scale=rstd_col(0, b))\
                        .then_inc(v_ready, 1)
                item0 = ITEM0[6 + half]
                for n, (h, segs) in enumerate(FORGET_ITEMS):
                    if n % TB == 0:
                        hh = 8 * half + h
                        act.wait_ge(cb_done, hh + 1)
                        if hh >= 2:
                            act.wait_ge(max_done, item0 + n - TB)
                        nc.scalar.activation(B_CB[:, hh % 2, :], PS[:, 2, :], ACT.Copy).then_inc(cb_ready, 1)
                    act.wait_ge(nm_ready, item0 + n + 1)
                    qb, kbs, c = segs[0]
                    w = slice(0, P * len(kbs))
                    nc.scalar.activation(B_P[:, n % 3, w], B_P[:, n % 3, w], ACT.Exp,
                                         bias=B_NM[:, 8 * half + h, qb:qb + 1],
                                         accum_out=B_DEN[:, 8 * half + h, qb:qb + 1]).then_inc(p_ready, 1)
            for t in range(DT):
                act.wait_ge(bc_used, 24 + t + 1)
                nc.scalar.activation(XH[:, t, :], B_Q[:, t % 2, :], ACT.Copy).then_inc(x_hi, 1)
            split(U["BO"] + 4, U["BO"] + 8)
            swiglu(1, 5, 3, 3, "ffn1")

            split(U["D1"] + 15, U["D1"] + 26)
            root(4)
            build_x(6, 5, "pre0", U["L"])
            act.wait_ge(ls_step, 1)
            nc.scalar.activation(L_S[:, 1, :], L_S[:, 0, :], ACT.Exp, scale=-1.0).then_inc(ls_exp, 1)
            root(5)
            for j in range(3):
                u = U["L"] + 8 * j
                split(u + 4, u + 8)
                for o in range(4):
                    c = 4 * j + o
                    act.wait_ge(xr_ready, c + 1)
                    if c >= 2:
                        act.wait_ge(cl_ready, c - 1)
                    nc.scalar.activation(L_XC[:, c % 2, :], L_XR[:, c % 2, 3:T + 3], ACT.Identity,
                                         scale=VC[:, VEC["conv3"] + c:VEC["conv3"] + c + 1],
                                         bias=VC[:, VEC["conv_b"] + c:VEC["conv_b"] + c + 1]).then_inc(xc_ready, 1)
                    act.wait_ge(conv_step, 3 * c + 3)
                    nc.scalar.activation(CH[:, c, :], L_XC[:, c % 2, :], ACT.Copy).then_inc(ch_ready, 1)
                split(u + 8, u + 12)
                for o in range(4):
                    c = 4 * j + o
                    act.wait_ge(lg_ready, c + 1)
                    if c >= 2:
                        act.wait_ge(lgs_ready, c - 1)
                    nc.scalar.activation(L_SG[:, c % 2, :], L_G[:, c, :], ACT.Sigmoid).then_inc(lsg_ready, 1)
            act.wait_ge(ls_ready, 1)
            for j in range(4):
                u = U["LG"] + 2 * j
                split(u + 4, u + 6)
                if j == 0:
                    act.wait_ge(lgs_ready, 12)
                    act.wait_ge(cl_ready, 12)
                else:
                    act.wait_ge(y_done, j)
                    act.wait_ge(h_done, 3 * j)
                for which, (dst, bias) in enumerate(((L_R, "b_a"), (L_I, "b_x"))):
                    act.wait_ge(unit_used, u + which + 1)
                    for o in range(3):
                        c = VEC[bias] + 3 * j + o
                        nc.scalar.activation(dst[:, o, :], PS[:, 4 * which + o, :], ACT.Sigmoid,
                                             bias=VC[:, c:c + 1]).then_inc(sig_done, 1)
                act.wait_ge(sig_done, 6 * j + 6)
                if j:
                    act.wait_ge(cl_ready, LT + 3 * j)
                for o in range(3):
                    c = 3 * j + o
                    nc.scalar.activation(L_A[:, o, :], L_R[:, o, :], ACT.Exp, scale=L_S[:, 5, c:c + 1])\
                        .then_inc(ae_done, 1)
                    nc.scalar.activation(L_E[:, o, :], L_R[:, o, :], ACT.Exp, scale=L_S[:, 6, c:c + 1])\
                        .then_inc(ae_done, 1)
                act.wait_ge(ae_done, 9 * j + 6)
                for o in range(3):
                    c = 3 * j + o
                    nc.scalar.activation(L_R[:, o, :], L_R[:, o, :], ACT.Tanh, scale=L_S[:, 7, c:c + 1])\
                        .then_inc(ae_done, 1)
                act.wait_ge(q_done, j + 1)
                nc.scalar.activation(L_E[:, :, :], L_E[:, :, :], ACT.Sqrt).then_inc(sqrt_done, 1)
                for o in range(3):
                    c = 3 * j + o
                    act.wait_ge(y_done, j + 1)
                    nc.scalar.activation(CH[:, c, :], L_A[:, o, :], ACT.Copy).then_inc(ch_ready, 1)
            split(U["LO"] + 4, U["LO"] + 10)
            for k in range(4):
                act.wait_ge(unit_used, U["LO"] + 6)
                if k == 0:
                    act.wait_ge(cl_ready, 2 * LT)
                nc.scalar.activation(L_O[:, k, :], PS[:, k, :], ACT.Copy).then_inc(lo_copied, 1)
            split(U["LO"] + 10, U["LO"] + 16)
            for k in range(4, 8):
                act.wait_ge(unit_used, U["LO"] + 12)
                nc.scalar.activation(L_O[:, k, :], PS[:, k, :], ACT.Copy).then_inc(lo_copied, 1)
            root(6)

            build_x(7, 6, "pre1", U["R"])
            act.wait_ge(post_mul, 8)
            act.dma_start(R_COS[:, :], turn_r[0]).then_inc(rotr_in, 16)
            act.dma_start(R_SIN[:, :], turn_r[1]).then_inc(rotr_in, 16)
            root(7, T + 4)
            for h in range(RH):
                u = U["R"] + 12 * h
                if h:
                    act.wait_ge(rpt_ready, 4 * h)
                else:
                    act.wait_ge(r_done, 56)
                act.dma_start(R_D[:, :], decay[h]).then_inc(decay_in, 16)
                split(u + 4, u + 12)
                act.wait_ge(unit_used, u + 8)
                act.wait_ge(rb_ready, 8)
                if h:
                    act.wait_ge(ro_done, 4 * h)
                for b in range(TB):
                    nc.scalar.activation(R_V[:, b, :], PS[:, 4 + b, :], ACT.Copy, scale=rstd_col(0, b))\
                        .then_inc(rv_ready, 1)
                split(u + 12, u + 16)
                act.wait_ge(unit_used, u + 12)
                act.wait_ge(rr_ready, 4 * h + 4)
                if h:
                    act.wait_ge(yt_done, 4 * h)
                for b in range(TB):
                    nc.scalar.activation(R_G[:, b, :], PS[:, b, :], ACT.Copy, scale=rstd_col(0, b))\
                        .then_inc(rg_ready, 1)
                    if 4 * h + b >= 2:
                        act.wait_ge(rgs_ready, 4 * h + b - 1)
                    nc.scalar.activation(R_SG[:, b % 2, :], PS[:, b, :], ACT.Sigmoid, scale=rstd_col(0, b))\
                        .then_inc(rsg_ready, 1)
                act.wait_ge(gn_step, 5 * h + 5)
                nc.scalar.activation(R_ST[:, 8:12], R_ST[:, 8:12], ACT.Sqrt).then_inc(gn_std, 1)
                act.wait_ge(gn_ready, h + 1)
                for b in range(TB):
                    if 4 * h + b >= 2:
                        act.wait_ge(ry_ready, 4 * h + b - 1)
                    nc.scalar.activation(R_SG[:, b % 2, :], PS[:, b, :], ACT.Identity, scale=R_ST[:, 12 + b:13 + b],
                                         bias=R_ST[:, 16 + b:17 + b]).then_inc(rn_ready, 1)
                for j in range(4):
                    act.wait_ge(yt_done, 4 * h + j + 1)
                    nc.scalar.activation(YH[:, 4 * h + j, :], PS[:, 4 + j, :], ACT.Copy).then_inc(yh_ready, 1)
            act.wait_ge(yl_ready, 16)
            act.dma_start(GAIN[:, :], post1.partition_broadcast(P)).then_inc(gain_in, 16)
            split(U["RO"] + 4, U["RO"] + 12)
            for d in range(2):
                act.wait_ge(unit_used, U["RO"] + 8 * (d + 1))
                for b in range(TB):
                    if 4 * d + b:
                        act.wait_ge(ss_done, 4 * d + b)
                    nc.scalar.activation(R_PT[:, 0:T], PS[:, 4 * d + b, :], ACT.Square,
                                         accum_out=R_ST[:, 4 * d + b:4 * d + b + 1]).then_inc(ss_done, 1)
                split(U["RO"] + 12, U["RO"] + 16) if d == 0 else None
            act.wait_ge(fin_step, 2)
            nc.scalar.activation(R_ST[:, 8:12], R_ST[:, 8:12], ACT.Sqrt).then_inc(fin_std, 1)

        @block.gpsimd
        def _(pool):
            def squares(s, src, ready):
                for k in range(DT):
                    ready(k)
                    if k == 0:
                        if s:
                            pool.wait_ge(stat_done, s)
                        nc.gpsimd.tensor_tensor(SQS[:, :], src[:, 0, :], src[:, 0, :], ALU.mult).then_inc(sq_mul, 1)
                        continue
                    if 7 * s + k - 1:
                        pool.wait_ge(sq_sum, 7 * s + k - 1)
                    nc.gpsimd.tensor_tensor(SQT[:, :], src[:, k, :], src[:, k, :], ALU.mult).then_inc(sq_mul, 1)
                    pool.wait_ge(sq_mul, 8 * s + k + 1)
                    nc.gpsimd.tensor_tensor(SQS[:, :], SQS[:, :], SQT[:, :], ALU.add).then_inc(sq_sum, 1)

            def residual(version):
                return lambda k: pool.wait_ge(r_done, 8 * version + k + 1)

            squares(0, R, residual(0))
            pool.wait_ge(tab_ready, 2)
            for m, (g, half) in enumerate(BODIES):
                for j in range(8):
                    r = 8 * m + j
                    dst = (A_Q if j < 4 else A_K)[:, j % 4, :]
                    pool.wait_ge(rot_sh, r + 1)
                    nc.gpsimd.tensor_tensor(A_SH[:, r % 2, :], A_SH[:, r % 2, :], A_SIN[:, :], ALU.mult)\
                        .then_inc(rot_m, 1)
                    pool.wait_ge(rot_a, r + 1)
                    pool.wait_ge(rot_m, r + 1)
                    if m and j == 0:
                        pool.wait_ge(s_done, ITEM0[m])
                    nc.gpsimd.tensor_tensor(by_step(dst, g), steps_of(A_T1[:, r % 2, :], g),
                                            steps_of(A_SH[:, r % 2, :], g), ALU.add).then_inc(qk_ready, 1)
            for t in range(DT):
                for i in range(2):
                    pool.wait_ge(bc_used, 3 * t + 2 + i)
                    if i:
                        pool.wait_ge(y_sum, 2 * t + 1)
                    elif t >= 2:
                        pool.wait_ge(x_lo, 8 + t - 1)
                    a = A_U[:, 0, :] if i == 0 else A_Y[:, t % 2, :]
                    nc.gpsimd.tensor_tensor(A_Y[:, t % 2, :], a, A_U[:, 1 + i, :], ALU.add).then_inc(y_sum, 1)

            def swiglu(layer, s, version):
                squares(s, R, residual(version))
                for j in range(11):
                    n = 11 * layer + j
                    pool.wait_ge(gs_ready, n + 1)
                    pool.wait_ge(u_ready, n + 1)
                    nc.gpsimd.tensor_tensor(F_U[:, :, :], F_G[:, :, :], F_U[:, :, :], ALU.mult).then_inc(ht_ready, 1)

            swiglu(0, 1, 1)
            squares(2, R, residual(2))
            swiglu(1, 3, 3)
            squares(4, R, residual(4))
            squares(5, R, residual(5))
            for c in range(LT):
                pool.wait_ge(lsg_ready, c + 1)
                nc.gpsimd.tensor_tensor(L_G[:, c, :], L_G[:, c, :], L_SG[:, c % 2, :], ALU.mult).then_inc(lgs_ready, 1)
            pool.wait_ge(cl_ready, 12)
            pool.wait_ge(ch_ready, 12)
            for j in range(4):
                if j:
                    pool.wait_ge(ix_done, j)
                else:
                    pool.wait_ge(lgs_ready, 12)
                tiles = slice(3 * j, 3 * j + 3)
                nc.gpsimd.tensor_tensor(L_X[:, :, :], CH[:, tiles, :].bitcast(F32), CL[:, tiles, :].bitcast(F32),
                                        ALU.add).then_inc(xs_done, 1)
                pool.wait_ge(xs_done, j + 1)
                pool.wait_ge(sig_done, 6 * j + 6)
                nc.gpsimd.tensor_tensor(L_I[:, :, :], L_I[:, :, :], L_X[:, :, :], ALU.mult).then_inc(ix_done, 1)
            squares(6, L_O, lambda k: pool.wait_ge(lo_copied, k + 1))
            squares(7, R, residual(6))
            for h in range(RH):
                for j in range(4):
                    pair, i = divmod(j, 2)
                    pool.wait_ge(rr_step, 4 * h + 2 * pair + 2)
                    if h and j == 0:
                        pool.wait_ge(rs_done, 4 * h)
                    nc.gpsimd.tensor_tensor(R_QK[:, j, :], R_T[0][:, i, :], R_T[1][:, 1 - i, :],
                                            ALU.subtract if i == 0 else ALU.add).then_inc(rr_ready, 1)

        @block.vector
        def _(dve):
            tt, stt, ts = nc.vector.tensor_tensor, nc.vector.scalar_tensor_tensor, nc.vector.tensor_scalar

            def split(a, b):
                for u in range(a, min(b, UNITS)):
                    s = u % RING
                    dve.wait_ge(hi_ready, u + 1)
                    tt(WL[:, s, :], WR[:, s, :], WH[:, s, :].bitcast(F32), ALU.subtract).then_inc(lo_ready, 1)

            def x_low(v, gain, k):
                dve.wait_ge(x_hi, 8 * v + k + 1)
                dve.wait_ge(r_done, 8 * VERSION[v] + k + 1)
                stt(XL[:, k, :], R[:, k, :], VC[:, VEC[gain] + k:VEC[gain] + k + 1], XH[:, k, :].bitcast(F32),
                    ALU.mult, ALU.subtract).then_inc(x_lo, 1)

            VERSION = {0: 0, 2: 1, 3: 2, 5: 3, 6: 5, 7: 6}

            def r_inc(ins):
                ins.then_inc(r_done, 1)

            def variance(s, bank, width=T):
                dve.wait_ge(stat_done, s + 1)
                v = PS[:, bank:bank + 2, :].rearrange("p b t -> p (b t)")
                ts(RB[:, 0:width], v[:, 0:width], 1.0 / D, RMS_EPS, ALU.mult, ALU.add).then_inc(rb_var, 1)

            def rstd(s, width=T):
                dve.wait_ge(rb_std, s + 1)
                nc.vector.reciprocal(RB[:, 0:width], RB[:, 0:width]).then_inc(rb_ready, 1)
                dve.wait_ge(rb_ready, s + 1)

            def add_out(v, gain, end, unit_step, late=False):
                for d in range(2):
                    if d:
                        split(*unit_step[1])
                    else:
                        split(*unit_step[0])
                    dve.wait_ge(unit_used, end[d])
                    for k in range(4 * d, 4 * d + 4):
                        r_inc(tt(R[:, k, :], R[:, k, :], PS[:, k, :], ALU.add))
                        if gain and k % 4 and not late:
                            x_low(v, gain, k - 1)
                    if gain and not late:
                        x_low(v, gain, 4 * d + 3)
                for k in range(DT if gain and late else 0):
                    x_low(v, gain, k)

            def scores_max(n, item0, segs, masks, PR, mx, nm):
                dve.wait_ge(s_done, item0 + n + 1)
                for qb, kbs, c in segs:
                    w = slice(c, c + P * len(kbs))
                    e = nc.vector.tensor_tensor_reduce(PR[:, n % 3, w], PS[:, 4 + n % 2, w], masks(kbs), HD ** -0.5,
                                                       3 * MASKED, ALU.add, ALU.max, mx(qb))
                e.then_inc(max_done, 1)
                dve.wait_ge(max_done, item0 + n + 1)
                ts(nm(slice(segs[0][0], segs[-1][0] + 1)), mx(slice(segs[0][0], segs[-1][0] + 1)), -1.0, None,
                   ALU.mult).then_inc(nm_ready, 1)

            def attention_tail(items, n, item0, PT, copy_out):
                m = n - 2
                if 0 <= m < len(items):
                    dve.wait_ge(t_done, item0 + m + 1)
                    if m >= 2:
                        dve.wait_ge(pv_done, item0 + m - 1)
                    w = width(items[m][1])
                    nc.vector.tensor_copy(PT[:, m % 2, 0:w], PS[:, 6 + m % 2, 0:w]).then_inc(pt_copied, 1)
                m = n - 3
                if 0 <= m < len(items):
                    h = items[m][0]
                    if h % 2 and (m == len(items) - 1 or items[m + 1][0] != h):
                        dve.wait_ge(pv_done, item0 + m + 1)
                        copy_out(h // 2)

            for k in range(DT):
                dve.wait_ge(x_turned, k + 1)
                r_inc(nc.vector.tensor_copy(R[:, k, :], PS[:, k, :]))
            split(0, 4)
            for k in range(DT):
                x_low(0, "a_norm", k)
            variance(0, 6, T + 12)
            rstd(0, T + 12)
            dve.wait_ge(rota_in, 32)
            tt(A_COS[:, :], A_COS[:, :], RB[:, 0:T], ALU.mult).then_inc(tab_ready, 1)
            tt(A_SIN[:, :], A_SIN[:, :], RB[:, 0:T], ALU.mult).then_inc(tab_ready, 1)
            dve.wait_ge(tab_ready, 2)
            swap = list(range(8, 16)) + list(range(8)) + list(range(16, 32))

            for m, (g, half) in enumerate(BODIES):
                u = U["A"] + 12 * m
                for part in range(2):
                    split(u + 4 + 4 * part, u + 8 + 4 * part)
                    dve.wait_ge(unit_used, u + 4 + 4 * part)
                    for j in range(4):
                        r = 8 * m + 4 * part + j
                        if r >= 2:
                            dve.wait_ge(qk_ready, r - 1)
                        tt(A_T1[:, r % 2, :], PS[:, 4 * part + j, :], A_COS[:, :], ALU.mult).then_inc(rot_a, 1)
                        nc.vector.stream_shuffle(A_SH[:, r % 2, :], PS[:, 4 * part + j, :], swap).then_inc(rot_sh, 1)
                split(u + 12, u + 16)
                items, item0 = ITEMS_A[g], ITEM0[m]

                def copy_out(t):
                    nc.vector.tensor_copy(by_class(A_O[:, g, 4 * half + t, :], g), classes_of(PS[:, t % 2, :], g))\
                        .then_inc(o_copied, 1)

                def masks(kbs):
                    if g == 0:
                        return CST[:, BAND + P * (2 - len(kbs)):BAND + 2 * P]
                    return CST[:, BAND + P:BAND + 2 * P] if g == 1 else CST[:, CLASS:CLASS + P]
                for n in range(len(items) + 4):
                    if n < len(items):
                        h, segs = items[n]
                        hh = 8 * half + h
                        scores_max(n, item0, segs, masks, A_P,
                                   lambda b: A_MX[:, g, hh, b] if isinstance(b, slice) else A_MX[:, g, hh, b:b + 1],
                                   lambda b: A_NM[:, g, hh, b])
                    attention_tail(items, n, item0, A_PT, copy_out)
            dve.wait_ge(st_turned, 1)
            for g in range(3):
                nc.vector.tensor_copy(by_class(A_MN[:, g, :], g), classes_of(PS[0:NH, g, :], g)).then_inc(st_copied, 1)
                nc.vector.tensor_copy(by_class(A_DN[:, g, :], g), classes_of(PS[0:NH, 3 + g, :], g))\
                    .then_inc(st_copied, 1)
            dve.wait_ge(st_copied, 6)
            tt(A_M[:, :], A_MN[:, 0, :], A_MN[:, 1, :], ALU.min).then_inc(st_step, 1)
            dve.wait_ge(st_step, 1)
            tt(A_M[:, :], A_M[:, :], A_MN[:, 2, :], ALU.min).then_inc(st_step, 1)
            dve.wait_ge(st_step, 2)
            for g in range(3):
                tt(A_MN[:, g, :], A_M[:, :], A_MN[:, g, :], ALU.subtract).then_inc(st_step, 1)
            dve.wait_ge(st_exp, 1)
            tt(A_DN[:, :, :], A_DN[:, :, :], A_MN[:, :, :], ALU.mult).then_inc(st_step, 1)
            dve.wait_ge(st_step, 6)
            tt(A_Z[:, :], A_DN[:, 0, :], A_DN[:, 1, :], ALU.add).then_inc(st_step, 1)
            dve.wait_ge(st_step, 7)
            tt(A_Z[:, :], A_Z[:, :], A_DN[:, 2, :], ALU.add).then_inc(st_copied, 1)
            dve.wait_ge(st_copied, 7)
            nc.vector.reciprocal(A_M[:, :], A_Z[:, :]).then_inc(st_copied, 1)
            dve.wait_ge(st_copied, 8)
            tt(A_MN[:, :, :], A_MN[:, :, :], A_M[:, :].unsqueeze(1).to_broadcast([NH, 3, T]), ALU.mult)\
                .then_inc(st_z, 1)
            for t in range(DT):
                for g in range(3):
                    n = 3 * t + g
                    dve.wait_ge(bc_done, n + 1)
                    if t:
                        dve.wait_ge(y_sum, 2 * t - 1 if g < 2 else 2 * t)
                    tt(A_U[:, g, :], A_O[:, g, t, :], PS[:, n % 8, :], ALU.mult).then_inc(bc_used, 1)
                if t:
                    dve.wait_ge(x_hi, 8 + t)
                    tt(XL[:, t - 1, :], A_Y[:, (t - 1) % 2, :], XH[:, t - 1, :].bitcast(F32), ALU.subtract)\
                        .then_inc(x_lo, 1)
            dve.wait_ge(x_hi, 16)
            tt(XL[:, 7, :], A_Y[:, 1, :], XH[:, 7, :].bitcast(F32), ALU.subtract).then_inc(x_lo, 1)
            ao = U["AO"]
            add_out(2, "ffn0", (ao + 4, ao + 8), ((ao + 4, ao + 8), (ao + 8, ao + 12)), True)

            def swiglu(layer, s):
                f, dn = U[f"F{layer}"], U[f"D{layer}"]
                variance(s, 0)
                rstd(s)
                rb2 = RB[:, 0:T].unsqueeze(1).to_broadcast([P, 2, T])

                def low(j):
                    dve.wait_ge(hh_ready, 11 * layer + j + 1)
                    tt(HL[:, 2 * j:2 * j + 2, :], F_U[:, :, :], HH[:, 2 * j:2 * j + 2, :].bitcast(F32),
                       ALU.subtract).then_inc(hl_ready, 1)
                for j in range(11):
                    n = 11 * layer + j
                    bank = 4 if j % 2 == 0 else 0
                    u = f + 4 * j
                    split(u + 4, u + 6)
                    if j:
                        low(j - 1)
                    split(u + 6, u + 8)
                    dve.wait_ge(unit_used, u + 4)
                    tt(F_G[:, :, :], PS[:, bank:bank + 2, :], rb2, ALU.mult).then_inc(g_ready, 1)
                    if j:
                        dve.wait_ge(hl_ready, n)
                    tt(F_U[:, :, :], PS[:, bank + 2:bank + 4, :], rb2, ALU.mult).then_inc(u_ready, 1)
                    dve.wait_ge(sg_ready, n + 1)
                    tt(F_G[:, :, :], F_G[:, :, :], F_S[:, :, :], ALU.mult).then_inc(gs_ready, 1)
                low(10)
                return dn

            dn = swiglu(0, 1)
            add_out(3, "b_norm", (dn + 11, dn + 22), ((dn + 4, dn + 15), (dn + 15, dn + 26)))

            variance(2, 6, T + 4)
            rstd(2, T + 4)
            dve.wait_ge(unit_used, U["BF"] + 1)
            tt(B_Z[:, :], PS[0:NH, 5, :], RB[0:NH, 0:T], ALU.mult).then_inc(lf_step, 1)
            split(U["BF"] + 4, U["BF"] + 5)
            count = [1]

            def step(ins):
                count[0] += 1
                ins.then_inc(lf_step, 1)
                dve.wait_ge(lf_step, count[0])
            dve.wait_ge(lf_step, 1)
            step(ts(B_Z[:, :], B_Z[:, :], VC[0:NH, VEC["b_f"]:VEC["b_f"] + 1], None, ALU.add))
            step(stt(B_A[:, :], B_Z[:, :], -1.0, B_Z[:, :], ALU.mult, ALU.max))
            dve.wait_ge(lf_exp, 1)

            def log1p_half(e, s, w, q, stp):
                stp(ts(w, e, 2.0, None, ALU.add))
                stp(nc.vector.reciprocal(w, w))
                stp(tt(s, e, w, ALU.mult))
                stp(tt(w, s, s, ALU.mult))
                stp(ts(q, w, 1.0 / 17, None, ALU.mult))
                for odd in (15, 13, 11, 9, 7, 5, 3):
                    stp(stt(q, q, 1.0 / odd, w, ALU.add, ALU.mult))
                stp(stt(q, q, 1.0, s, ALU.add, ALU.mult))
            log1p_half(B_E[:, :], B_S[:, :], B_W[:, :], B_A[:, :], step)
            step(ts(B_Z[:, :], B_Z[:, :], 0.0, None, ALU.min))
            step(stt(B_A[:, :], B_A[:, :], 2.0, B_Z[:, :], ALU.mult, ALU.subtract))
            step(ts(B_A[:, :], B_A[:, :], 8.0, None, ALU.mult))
            step(nc.vector.memset(B_1[:, :], 1.0))
            nc.vector.tensor_tensor_scan(B_NC[:, :], B_1[:, :], B_A[:, :], 0.0, ALU.mult, ALU.add)\
                .then_inc(nc_ready, 1)

            for half in range(2):
                u = U["B"] + 12 * half
                for part in range(2):
                    split(u + 4 + 4 * part, u + 8 + 4 * part)
                    dve.wait_ge(unit_used, u + 4 + 4 * part)
                    if half:
                        dve.wait_ge(s_done, ITEM0[7])
                    for j in range(4):
                        tt((B_K if part else B_Q)[:, j, :], PS[:, 4 * part + j, :], RB[:, 0:T], ALU.mult)\
                            .then_inc(bq_ready, 1)
                split(u + 12, u + 16)
                item0 = ITEM0[6 + half]

                def copy_out(t):
                    nc.vector.tensor_copy(B_O[:, 4 * half + t, :], PS[:, t % 2, :]).then_inc(o_copied, 1)
                for n in range(len(FORGET_ITEMS) + 4):
                    if n < len(FORGET_ITEMS):
                        h, segs = FORGET_ITEMS[n]
                        hh = 8 * half + h
                        qb = segs[0][0]
                        if qb == 0:
                            dve.wait_ge(cb_ready, hh + 1)
                            tt(B_DG[:, hh % 2, :].rearrange("p (b t) -> p b t", b=TB),
                               B_CB[:, hh % 2, :].rearrange("p (b t) -> p b t", b=TB),
                               CST[:, BAND + P:BAND + 2 * P].unsqueeze(1).to_broadcast([P, TB, P]), ALU.add)\
                                .then_inc(dg_ready, 1)
                            dve.wait_ge(dg_ready, hh + 1)
                        dve.wait_ge(s_done, item0 + n + 1)
                        own = slice(qb * P, (qb + 1) * P)
                        ttr = nc.vector.tensor_tensor_reduce
                        if qb:
                            w = slice(0, qb * P)
                            ttr(B_P[:, n % 3, w], PS[:, 4 + n % 2, w], B_CB[:, hh % 2, w], HD ** -0.5, 3 * MASKED,
                                ALU.add, ALU.max, B_MX[:, hh, qb, 1:2])
                        ttr(B_P[:, n % 3, own], PS[:, 4 + n % 2, own], B_DG[:, hh % 2, own], HD ** -0.5, 3 * MASKED,
                            ALU.add, ALU.max, B_MX[:, hh, qb, 0:1]).then_inc(max_done, 1)
                        dve.wait_ge(max_done, item0 + n + 1)
                        if qb:
                            ts(B_NM[:, hh, qb:qb + 1], B_MX[:, hh, qb, 0:1], B_MX[:, hh, qb, 1:2], -1.0,
                               ALU.max, ALU.mult).then_inc(nm_ready, 1)
                        else:
                            ts(B_NM[:, hh, qb:qb + 1], B_MX[:, hh, qb, 0:1], -1.0, None, ALU.mult)\
                                .then_inc(nm_ready, 1)
                    attention_tail(FORGET_ITEMS, n, item0, B_PT, copy_out)
            dve.wait_ge(p_ready, ITEM0[8])
            nc.vector.reciprocal(B_DEN[:, :, :], B_DEN[:, :, :]).then_inc(st_step, 1)
            dve.wait_ge(st_turned, 2)
            nc.vector.tensor_copy(B_RD[:, :], PS[0:NH, 0, :]).then_inc(st_z, 1)
            for t in range(DT):
                dve.wait_ge(bc_done, 24 + t + 1)
                if t >= 2:
                    dve.wait_ge(x_lo, 8 * 4 + t - 1)
                tt(B_Q[:, t % 2, :], B_O[:, t, :], PS[:, 4 + t % 4, :], ALU.mult).then_inc(bc_used, 1)
                dve.wait_ge(x_hi, 8 * 4 + t + 1)
                tt(XL[:, t, :], B_Q[:, t % 2, :], XH[:, t, :].bitcast(F32), ALU.subtract).then_inc(x_lo, 1)
            bo = U["BO"]
            add_out(5, "ffn1", (bo + 4, bo + 8), ((bo + 4, bo + 8), (bo + 8, bo + 12)), True)

            dn = swiglu(1, 3)
            add_out(None, None, (dn + 11, dn + 22), ((dn + 4, dn + 15), (dn + 15, dn + 26)))
            variance(4, 6)
            rstd(4)
            for k in range(DT):
                c = VEC["final"] + k
                r_inc(stt(R[:, k, :], R[:, k, :], VC[:, c:c + 1], RB[:, 0:T], ALU.mult, ALU.mult))

            count = [0]

            def lstep(ins):
                count[0] += 1
                ins.then_inc(ls_step, 1)
                dve.wait_ge(ls_step, count[0])
            lam = VC[:, VEC["lam"]:VEC["lam"] + LT]
            lstep(stt(L_S[:, 0, :], lam, -1.0, lam, ALU.mult, ALU.max))
            for k in range(DT):
                x_low(6, "pre0", k)
            dve.wait_ge(ls_exp, 1)
            log1p_half(L_S[:, 1, :], L_S[:, 2, :], L_S[:, 3, :], L_S[:, 4, :], lstep)
            lstep(ts(L_S[:, 2, :], lam, 0.0, None, ALU.min))
            lstep(stt(L_S[:, 3, :], L_S[:, 4, :], 2.0, L_S[:, 2, :], ALU.mult, ALU.subtract))
            lstep(ts(L_S[:, 5, :], L_S[:, 3, :], -8.0, None, ALU.mult))
            lstep(ts(L_S[:, 6, :], L_S[:, 3, :], -16.0, None, ALU.mult))
            ts(L_S[:, 7, :], L_S[:, 3, :], 8.0, None, ALU.mult).then_inc(ls_ready, 1)
            variance(5, 6)
            rstd(5)
            nc.vector.memset(L_XR[:, :, 0:3], 0.0).then_inc(ls_ready, 1)
            dve.wait_ge(ls_ready, 2)

            def convolve(c):
                for i in range(3):
                    dve.wait_ge(xc_ready, c + 1)
                    if i:
                        dve.wait_ge(conv_step, 3 * c + i)
                    w = VEC[f"conv{i}"] + c
                    stt(L_XC[:, c % 2, :], L_XR[:, c % 2, i:i + T], VC[:, w:w + 1], L_XC[:, c % 2, :],
                        ALU.mult, ALU.add).then_inc(conv_step, 1)

            def conv_low(c):
                dve.wait_ge(ch_ready, c + 1)
                tt(CL[:, c, :], L_XC[:, c % 2, :], CH[:, c, :].bitcast(F32), ALU.subtract).then_inc(cl_ready, 1)
            for j in range(3):
                u = U["L"] + 8 * j
                split(u + 4, u + 8)
                dve.wait_ge(unit_used, u + 4)
                for o in range(4):
                    c = 4 * j + o
                    tt(L_XR[:, c % 2, 3:T + 3], PS[:, o, :], RB[:, 0:T], ALU.mult).then_inc(xr_ready, 1)
                    if o:
                        convolve(c - 1)
                        conv_low(c - 1)
                convolve(4 * j + 3)
                conv_low(4 * j + 3)
                split(u + 8, u + 12)
                dve.wait_ge(unit_used, u + 8)
                for o in range(4):
                    tt(L_G[:, 4 * j + o, :], PS[:, 4 + o, :], RB[:, 0:T], ALU.mult).then_inc(lg_ready, 1)
            for j in range(4):
                u = U["LG"] + 2 * j
                split(u + 4, u + 6)
                dve.wait_ge(ae_done, 9 * j + 9)
                stt(L_E[:, :, :], L_E[:, :, :], 1.0, L_R[:, :, :], ALU.add, ALU.mult).then_inc(q_done, 1)
                dve.wait_ge(ix_done, j + 1)
                dve.wait_ge(sqrt_done, j + 1)
                tt(L_I[:, :, :], L_I[:, :, :], L_E[:, :, :], ALU.mult).then_inc(bt_done, 1)
                dve.wait_ge(bt_done, j + 1)
                for o in range(3):
                    nc.vector.tensor_tensor_scan(L_R[:, o, :], L_A[:, o, :], L_I[:, o, :], 0.0, ALU.mult, ALU.add)\
                        .then_inc(h_done, 1)
                dve.wait_ge(h_done, 3 * j + 3)
                dve.wait_ge(lgs_ready, LT)
                tt(L_A[:, :, :], L_R[:, :, :], L_G[:, 3 * j:3 * j + 3, :], ALU.mult).then_inc(y_done, 1)
                for o in range(3):
                    c = 3 * j + o
                    dve.wait_ge(ch_ready, LT + c + 1)
                    tt(CL[:, c, :], L_A[:, o, :], CH[:, c, :].bitcast(F32), ALU.subtract).then_inc(cl_ready, 1)
            split(U["LO"] + 4, U["LO"] + 16)
            variance(6, 6)
            rstd(6)
            for k in range(DT):
                c = VEC["post0"] + k
                stt(L_O[:, k, :], L_O[:, k, :], VC[:, c:c + 1], RB[:, 0:T], ALU.mult, ALU.mult).then_inc(post_mul, 1)
                dve.wait_ge(post_mul, k + 1)
                r_inc(tt(R[:, k, :], R[:, k, :], L_O[:, k, :], ALU.add))
                if k:
                    x_low(7, "pre1", k - 1)
            x_low(7, "pre1", 7)

            variance(7, 6, T + 4)
            rstd(7, T + 4)
            dve.wait_ge(rotr_in, 32)
            tt(R_COS[:, :], R_COS[:, :], RB[:, 0:T], ALU.mult).then_inc(tab_ready, 1)
            tt(R_SIN[:, :], R_SIN[:, :], RB[:, 0:T], ALU.mult).then_inc(tab_ready, 1)
            dve.wait_ge(tab_ready, 4)
            cos2 = R_COS[:, :].unsqueeze(1).to_broadcast([P, 2, T])
            sin2 = R_SIN[:, :].unsqueeze(1).to_broadcast([P, 2, T])
            for h in range(RH):
                u = U["R"] + 12 * h
                split(u + 4, u + 8)
                dve.wait_ge(unit_used, u + 4)
                for pair in range(2):
                    if pair:
                        dve.wait_ge(rr_ready, 4 * h + 2)
                    elif h:
                        dve.wait_ge(yt_done, 4 * h)
                    tt(R_T[0][:, :, :], PS[:, 2 * pair:2 * pair + 2, :], cos2, ALU.mult).then_inc(rr_step, 1)
                    tt(R_T[1][:, :, :], PS[:, 2 * pair:2 * pair + 2, :], sin2, ALU.mult).then_inc(rr_step, 1)
                split(u + 8, u + 16)
                for b in range(TB):
                    dve.wait_ge(rsg_ready, 4 * h + b + 1)
                    dve.wait_ge(rg_ready, 4 * h + b + 1)
                    tt(R_G[:, b, :], R_G[:, b, :], R_SG[:, b % 2, :], ALU.mult).then_inc(rgs_ready, 1)
                dve.wait_ge(decay_in, 16 * (h + 1))
                for kb in range(TB):
                    dve.wait_ge(rs_done, 4 * h + kb + 1)
                    if h and kb == 0:
                        dve.wait_ge(ro_done, 4 * h)
                    w = T - kb * P
                    tt(R_PT[:, PT0[kb]:PT0[kb] + w], PS[:, 4 + kb, 0:w], R_D[:, 0:w], ALU.mult).then_inc(rpt_ready, 1)
                for b in range(TB):
                    dve.wait_ge(ro_done, 4 * h + b + 1)
                    nc.vector.bn_stats(R_ST[:, 20 + 6 * b:26 + 6 * b], PS[:, b, :]).then_inc(gn_step, 1)
                    dve.wait_ge(gn_step, 5 * h + b + 1)
                    nc.vector.bn_aggr(R_ST[:, 2 * b:2 * b + 2], R_ST[:, 20 + 6 * b:26 + 6 * b]).then_inc(rr_bn, 1)
                dve.wait_ge(rr_bn, 4 * h + 4)
                st = R_ST[:, 0:8].rearrange("p (b i) -> p b i", i=2)
                ts(R_ST[:, 8:12], st[:, :, 1], GN_EPS, None, ALU.add).then_inc(gn_step, 1)
                dve.wait_ge(gn_std, h + 1)
                nc.vector.reciprocal(R_ST[:, 12:16], R_ST[:, 8:12]).then_inc(gn_r, 1)
                dve.wait_ge(gn_r, h + 1)
                stt(R_ST[:, 16:20], st[:, :, 0], -1.0, R_ST[:, 12:16], ALU.mult, ALU.mult).then_inc(gn_ready, 1)
                for b in range(TB):
                    dve.wait_ge(rn_ready, 4 * h + b + 1)
                    dve.wait_ge(rgs_ready, 4 * h + b + 1)
                    tt(R_G[:, b, :], R_G[:, b, :], R_SG[:, b % 2, :], ALU.mult).then_inc(ry_ready, 1)
                for j in range(4):
                    dve.wait_ge(yt_done, 4 * h + j + 1)
                    dve.wait_ge(yh_ready, 4 * h + j + 1)
                    tt(YL[:, 4 * h + j, :], PS[:, 4 + j, :], YH[:, 4 * h + j, :].bitcast(F32), ALU.subtract)\
                        .then_inc(yl_ready, 1)
            for b in range(TB):
                dve.wait_ge(rt_turned, b + 1)
                bank = 2 * (b % 2)
                nc.vector.tensor_copy(OUT[:, b, :], PS[:, bank:bank + 2, :].rearrange("p b t -> p (b t)"))\
                    .then_inc(rt_ready, 1)
            split(U["RO"] + 4, U["RO"] + 16)
            dve.wait_ge(ss_done, 8)
            tt(R_ST[:, 8:12], R_ST[:, 0:4], R_ST[:, 4:8], ALU.add).then_inc(fin_step, 1)
            dve.wait_ge(fin_step, 1)
            ts(R_ST[:, 8:12], R_ST[:, 8:12], 1.0 / D, RMS_EPS, ALU.mult, ALU.add).then_inc(fin_step, 1)
            dve.wait_ge(fin_std, 1)
            nc.vector.reciprocal(R_ST[:, 12:16], R_ST[:, 8:12]).then_inc(fin_step, 1)
            dve.wait_ge(fin_step, 3)
            dve.wait_ge(gain_in, 16)
            for b in range(TB):
                for d in range(2):
                    w = slice(T * d, T * d + T)
                    i = 2 * b + d
                    stt(R_TF[:, i % 2, :], PS[:, 4 * d + b, :], R_ST[:, 12 + b:13 + b], GAIN[:, w],
                        ALU.mult, ALU.mult).then_inc(o_scaled, 1)
                    dve.wait_ge(o_scaled, i + 1)
                    e = tt(OUT[:, b, w], OUT[:, b, w], R_TF[:, i % 2, :], ALU.add)
                    if d:
                        e.then_inc(o_ready, 1)


def rotary_tables():
    f32 = np.float32
    pos = np.arange(T, dtype=f32)
    inv = f32(500000.0) ** (-np.arange(8, dtype=f32) * f32(2.0) / f32(16.0))
    ang = (pos[None, :] * inv[:, None]).astype(f32)
    cos, sin = np.ones((2, HD, T), f32), np.zeros((2, HD, T), f32)
    cos[:, 0:8] = cos[:, 8:16] = np.cos(ang)
    sin[:, 0:8], sin[:, 8:16] = -np.sin(ang), np.sin(ang)
    a = np.stack([cos.reshape(P, T), sin.reshape(P, T)])
    inv = f32(10000.0) ** (-np.arange(0, 256, 2, dtype=f32) / f32(256))
    ang = (pos[None, :] * inv[:, None]).astype(f32)
    return a, np.stack([np.cos(ang), np.sin(ang)]).astype(f32)


def constant_table():
    i = np.arange(P)
    c = np.zeros((P, NCST), np.float32)
    c[:, IDENT:IDENT + P] = np.eye(P)
    c[:, ONES:ONES + P] = 1.0
    q, k = i[:, None], i[None, :]
    c[:, BAND:BAND + P] = np.where(k >= q, 0.0, MASKED)
    c[:, BAND + P:BAND + 2 * P] = np.where(k <= q, 0.0, MASKED)
    c[:, CLASS:CLASS + P] = np.where((k <= q) & (k % 4 == q % 4), 0.0, MASKED)
    return c


def decay_table():
    g = 1.0 - 2.0 ** (-5.0 - np.arange(RH, dtype=np.float64))
    diff = np.arange(T)[None, :] - np.arange(P)[:, None]
    return np.where(diff >= 0, g[:, None, None] ** np.maximum(diff, 0) / 16.0, 0.0).astype(np.float32)


def units(w):
    k, n = w.shape
    return w.reshape(k // 256, 2, P, n // 512, 512).transpose(3, 0, 2, 1, 4).reshape(-1, P, UNIT)


def kernel(**inputs):
    import concourse.bacc as _bacc
    from concourse.bass_utils import run_bass_kernel_spmd as _run

    v = {k: np.asarray(a) for k, a in inputs.items()}
    f32 = np.float32

    def gate_up(i):
        w = v["ffn_w_gu"][i].reshape(D, 2, 11, 256)
        return np.ascontiguousarray(w.transpose(0, 2, 1, 3)).reshape(D, 22 * 256)

    a_in = v["a_w_in"][0].reshape(D, 3, 3, 2, 512).transpose(0, 1, 3, 2, 4).reshape(D, -1)
    b_in = v["b_w_in"][0][:, :3072].reshape(D, 3, 2, 512).transpose(0, 2, 1, 3).reshape(D, -1)
    forget = np.zeros((DT, P, P), f32)
    forget[:, :, :NH] = v["b_w_in"][0][:, 3072:].reshape(DT, P, NH)
    forget = forget.transpose(1, 0, 2).reshape(1, P, UNIT)
    l_in = v["lru_w_in_2"][0].reshape(D, 2, 3, 512).transpose(0, 2, 1, 3).reshape(D, -1)
    gates = np.zeros((4, 2, P, UNIT), f32)
    for j in range(4):
        for which, name in enumerate(("lru_w_a_2", "lru_w_x_2")):
            full = np.zeros((384, 384), f32)
            for b in range(4):
                full[96 * b:96 * b + 96, 96 * b:96 * b + 96] = v[name][0, 4 * j + b]
            for n, (i, o) in enumerate(GATE_BLOCKS):
                gates[j, which, :, n * P:(n + 1) * P] = full[i * P:(i + 1) * P, o * P:(o + 1) * P]
    rw = v["ret_w_in_2"][0]
    r_in = np.concatenate([np.concatenate([
        rw[:, 256 * h:256 * h + 256], rw[:, 1024 + 256 * h:1280 + 256 * h],
        rw[:, 2048 + 512 * h:2560 + 512 * h], rw[:, 4096 + 512 * h:4608 + 512 * h]], axis=1) for h in range(RH)],
        axis=1)
    ws = np.concatenate([
        units(a_in), units(v["a_w_out"][0]), units(gate_up(0)), units(v["ffn_w_down"][0]),
        forget, units(b_in), units(v["b_w_out"][0]), units(gate_up(1)), units(v["ffn_w_down"][1]),
        units(l_in), gates.reshape(8, P, UNIT), units(v["lru_w_out_2"][0]),
        units(r_in), units(v["ret_w_out_2"][0])])
    assert ws.shape[0] == UNITS

    vec = np.zeros((P, NVEC), f32)

    def column(name, a):
        a = a.reshape(-1, P).T
        vec[:, VEC[name]:VEC[name] + a.shape[1]] = a
    for name, a in (("a_norm", v["a_norm"][0]), ("ffn0", v["ffn_norm"][0]), ("b_norm", v["b_norm"][0]),
                    ("ffn1", v["ffn_norm"][1]), ("final", v["final_norm"]), ("pre0", v["norm_pre_2"][0]),
                    ("post0", v["norm_post_2"][0]), ("pre1", v["norm_pre_2"][1]), ("conv_b", v["lru_conv_b_2"][0]),
                    ("b_a", v["lru_b_a_2"][0]), ("b_x", v["lru_b_x_2"][0]), ("lam", v["lru_lambda_2"][0])):
        column(name, a)
    for i in range(4):
        column(f"conv{i}", v["lru_conv_w_2"][0, i])
    vec[:NH, VEC["b_f"]] = v["b_f"][0]
    turn_a, turn_r = rotary_tables()

    arrays = {"ws": ws, "x": v["x"][0], "vec": vec, "cst": constant_table(),
              "sel": np.repeat(np.eye(NH, dtype=f32), HD, axis=1), "turn_a": turn_a, "turn_r": turn_r,
              "decay": decay_table(), "post1": v["norm_post_2"][1]}
    arrays = {k: np.ascontiguousarray(a) for k, a in arrays.items()}
    nc = _bacc.Bacc("TRN2", target_bir_lowering=False, num_devices=1)
    args = [nc.dram_tensor(f"in_{k}", a.shape, F32, kind="ExternalInput").ap() for k, a in arrays.items()]
    shape = (T, D)
    args.append(nc.dram_tensor("out_0", shape, F32, kind="ExternalOutput").ap())
    program(nc, *args)
    r = _run(nc, [{f"in_{k}": a for k, a in arrays.items()}], core_ids=[0])
    return r.results[0]["out_0"].reshape(1, T, D)
```

```python
from contextlib import ExitStack

import numpy as np
import concourse.bass as bass
from concourse import mybir

F32 = mybir.dt.float32
F32R = mybir.dt.float32r
ALU = mybir.AluOpType
ACT = mybir.ActivationFunctionType
AX = mybir.AxisListType

P = 128
T = 512
TB = T // P
D = 1024
DT = D // P
NH = 16
HD = 64
FT = 22
LT = 12
RH = 4
RMS_EPS = 1e-6
GN_EPS = 1e-5
MASKED = -1e30
RING = 4
UNIT = 8 * P

PHASES = [("A", 72), ("AO", 8), ("F0", 44), ("D0", 22), ("BF", 1), ("B", 24), ("BO", 8), ("F1", 44),
          ("D1", 22), ("L", 24), ("LG", 8), ("LO", 12), ("R", 48), ("RO", 16)]
START = {}
_n = 0
for _name, _count in PHASES:
    START[_name] = _n
    _n += _count
UNITS = _n

VEC = {}
_n = 0
for _name, _count in [("a_norm", 8), ("ffn0", 8), ("b_norm", 8), ("ffn1", 8), ("final", 8), ("pre0", 8),
                      ("post0", 8), ("pre1", 8), ("conv0", LT), ("conv1", LT), ("conv2", LT), ("conv3", LT),
                      ("conv_b", LT), ("b_a", LT), ("b_x", LT), ("lam", LT), ("b_f", 1)]:
    VEC[_name] = _n
    _n += _count
NVEC = _n
IDENT, ONES, BAND, CLASS, NCST = 0, 128, 256, 512, 640
GATE_BLOCKS = [(0, 0), (1, 0), (0, 1), (1, 1), (2, 1), (1, 2), (2, 2)]


def program(nc, ws, x, vec, cst, sel, turn_a, turn_r, decay, post1, out):
    with ExitStack() as ctx:
        def sem(name):
            return ctx.enter_context(nc.semaphore(name))

        top = [nc.sbuf_base + (-nc.sbuf_base) % 32]

        def sb(name, shape, dt=F32, at=None):
            size = int(np.prod(shape[1:])) * 4
            where = top[0] if at is None else at
            t = nc.alloc_sbuf_tensor_at(name, shape, dt, offset=where)
            if at is None:
                top[0] += size + (-size) % 32
            return t

        R = sb("R", [P, DT, T])
        operand_at = top[0]
        XH = sb("XH", [P, DT, T], F32R)
        XL = sb("XL", [P, DT, T], F32R)
        WR = sb("WR", [P, RING, UNIT])
        WH = sb("WH", [P, RING, UNIT], F32R)
        WL = sb("WL", [P, RING, UNIT], F32R)
        VC = sb("VC", [P, NVEC])
        GV = sb("GV", [P, 2, DT])
        CST = sb("CST", [P, NCST])
        RB = sb("RB", [P, T + 16])
        squares_at = top[0]
        SQT = sb("SQT", [P, T])
        SQS = sb("SQS", [P, T])
        arena = top[0]
        limit = nc.sbuf_usable_end

        class Arena:
            def __init__(self):
                self.at = arena

            def __call__(self, name, shape, dt=F32):
                t = sb(name, shape, dt, at=self.at)
                size = int(np.prod(shape[1:])) * 4
                self.at += size + (-size) % 32
                assert self.at <= limit, (name, self.at - limit)
                return t

        a = Arena()
        A_Q = a("A_Q", [P, 4, T])
        A_K = a("A_K", [P, 4, T])
        A_V = a("A_V", [P, TB, T])
        A_O = a("A_O", [P, 3, DT, T])
        A_COS = a("A_COS", [P, T])
        A_SIN = a("A_SIN", [P, T])
        A_P = a("A_P", [P, 3, T])
        A_PT = a("A_PT", [P, 2, T])
        A_T1 = a("A_T1", [P, 2, T])
        A_SH = a("A_SH", [P, 2, T])
        A_MX = a("A_MX", [P, 3, NH, TB])
        A_NM = a("A_NM", [P, 3, NH, TB])
        A_DEN = a("A_DEN", [P, 3, NH, TB])
        A_SEL = a("A_SEL", [NH, D])
        XTOK = sb("XTOK", [P, TB, D], at=arena)
        a = Arena()
        A_MN = a("A_MN", [NH, 3, T])
        A_DN = a("A_DN", [NH, 3, T])
        A_M = a("A_M", [NH, T])
        A_Z = a("A_Z", [NH, T])
        A_Y = a("A_Y", [P, 2, T])
        A_SR = a("A_SR", [NH, D], F32R)
        A_ML = sb("A_ML", [NH, 3, T], F32R, at=arena + 3 * T * 4)
        A_MH = sb("A_MH", [NH, 3, T], F32R, at=arena + 3 * 8192 + 3 * 16384 + 4096 + 6144 + 4096)
        A_U = sb("A_U", [P, 3, T], at=arena + 3 * 8192 + 3 * 16384 + 4096)
        a = Arena()
        HH = a("HH", [P, FT, T], F32R)
        HL = a("HL", [P, FT, T], F32R)
        F_G = a("F_G", [P, 2, T])
        F_U = a("F_U", [P, 2, T])
        F_S = a("F_S", [P, 2, T])
        a = Arena()
        B_Q = a("B_Q", [P, 4, T])
        B_K = a("B_K", [P, 4, T])
        B_V = a("B_V", [P, TB, T])
        B_O = a("B_O", [P, DT, T])
        B_CB = a("B_CB", [P, 2, T])
        B_DG = a("B_DG", [P, 2, T])
        B_P = a("B_P", [P, 3, T])
        B_PT = a("B_PT", [P, 2, T])
        B_MX = a("B_MX", [P, NH, TB, 2])
        B_NM = a("B_NM", [P, NH, TB])
        B_DEN = a("B_DEN", [P, NH, TB])
        B_SEL = a("B_SEL", [NH, D])
        B_RD = a("B_RD", [NH, T])
        B_NC = a("B_NC", [NH, T])
        B_Z = a("B_Z", [NH, T])
        B_E = a("B_E", [NH, T])
        B_S = a("B_S", [NH, T])
        B_W = a("B_W", [NH, T])
        B_A = a("B_A", [NH, T])
        B_1 = a("B_1", [NH, T])
        a = Arena()
        CH = a("CH", [P, LT, T], F32R)
        CL = a("CL", [P, LT, T], F32R)
        L_G = a("L_G", [P, LT, T])
        L_R = a("L_R", [P, 3, T])
        L_I = a("L_I", [P, 3, T])
        L_A = a("L_A", [P, 3, T])
        L_E = a("L_E", [P, 3, T])
        L_X = a("L_X", [P, 3, T])
        L_S = a("L_S", [P, 8, LT])
        tmp = arena + 4 * LT * T * 3
        L_XR = sb("L_XR", [P, 2, T + 3 + 1], at=tmp)
        L_XC = sb("L_XC", [P, 2, T], at=tmp + 4160)
        L_SG = sb("L_SG", [P, 2, T], at=tmp + 4160 + 4096)
        L_O = sb("L_O", [P, DT, T], at=tmp)
        def pair_of(t, name, n):
            return [t[:, :, :], sb(name, [P, 3, T], at=operand_at + 3 * T * 4 * n)[:, :, :]]
        L_R2, L_I2, L_A2, L_E2 = [pair_of(t, name, n) for n, (t, name) in enumerate(
            [(L_R, "L_RB"), (L_I, "L_IB"), (L_A, "L_AB"), (L_E, "L_EB")])]
        a = Arena()
        YH = a("YH", [P, 16, T], F32R)
        YL = a("YL", [P, 16, T], F32R)
        R_QK = a("R_QK", [P, 4, T])
        R_V = a("R_V", [P, TB, T])
        R_G = a("R_G", [P, TB, T])
        R_PT = a("R_PT", [P, 1280])
        R_D = a("R_D", [P, T])
        R_COS = a("R_COS", [P, T])
        R_SIN = a("R_SIN", [P, T])
        R_SG = sb("R_SG", [P, 2, T], at=squares_at)
        R_ST = a("R_ST", [P, 64])
        base_qk = arena + 2 * 16 * T * 4
        OUT = sb("OUT", [P, TB, D], at=base_qk)
        GAIN = sb("GAIN", [P, D], at=base_qk + 16384)
        R_T = [sb("R_T1", [P, 2, T], at=base_qk + 16384), sb("R_T2", [P, 2, T], at=base_qk + 16384 + 4096)]

        PS = ctx.enter_context(nc.psum_tensor("PS", [P, 8, 512], F32))

        ident = CST[:, IDENT:IDENT + P]
        ones = CST[:, ONES:ONES + P]

        landed = [sem(f"landed{i}") for i in range(RING)]
        hi_ready = sem("hi_ready")
        lo_ready = sem("lo_ready")
        unit_used = sem("unit_used")
        consts_in, x_in, rota_in, rotr_in, gain_in, decay_in, sel_in = (
            sem("consts_in"), sem("x_in"), sem("rota_in"), sem("rotr_in"), sem("gain_in"), sem("decay_in"),
            sem("sel_in"))
        x_turned = sem("x_turned")
        r_done = sem("r_done")
        x_hi, x_lo = sem("x_hi"), sem("x_lo")
        sq_mul, sq_sum = sem("sq_mul"), sem("sq_sum")
        stat_done, rb_var, rb_std, rb_ready = sem("stat_done"), sem("rb_var"), sem("rb_std"), sem("rb_ready")
        tab_ready = sem("tab_ready")
        rot_a, rot_sh, rot_m, qk_ready, v_ready = (
            sem("rot_a"), sem("rot_sh"), sem("rot_m"), sem("qk_ready"), sem("v_ready"))
        s_done, max_done, nm_ready, p_ready = sem("s_done"), sem("max_done"), sem("nm_ready"), sem("p_ready")
        t_done, pt_copied, pv_done, o_copied = sem("t_done"), sem("pt_copied"), sem("pv_done"), sem("o_copied")
        st_turned, st_copied, st_step, st_exp, st_z = (
            sem("st_turned"), sem("st_copied"), sem("st_step"), sem("st_exp"), sem("st_z"))
        bc_done, bc_used, y_sum = sem("bc_done"), sem("bc_used"), sem("y_sum")
        g_ready, u_ready, sg_ready, gs_ready, ht_ready, hh_ready, hl_ready = (
            sem("g_ready"), sem("u_ready"), sem("sg_ready"), sem("gs_ready"), sem("ht_ready"), sem("hh_ready"),
            sem("hl_ready"))
        fz_done, lf_step, lf_exp, nc_ready, cb_done, cb_ready, dg_ready = (
            sem("fz_done"), sem("lf_step"), sem("lf_exp"), sem("nc_ready"), sem("cb_done"), sem("cb_ready"),
            sem("dg_ready"))
        bq_ready = sem("bq_ready")
        xr_ready, xc_ready, conv_step, ch_ready, cl_ready = (
            sem("xr_ready"), sem("xc_ready"), sem("conv_step"), sem("ch_ready"), sem("cl_ready"))
        lg_ready, lsg_ready, lgs_ready = sem("lg_ready"), sem("lsg_ready"), sem("lgs_ready")
        ls_step, ls_exp, ls_ready = sem("ls_step"), sem("ls_exp"), sem("ls_ready")
        sig_done, ae_done, q_done, sqrt_done, xs_done, ix_done, bt_done, h_done, y_done = (
            sem("sig_done"), sem("ae_done"), sem("q_done"), sem("sqrt_done"), sem("xs_done"), sem("ix_done"),
            sem("bt_done"), sem("h_done"), sem("y_done"))
        lo_copied, post_mul = sem("lo_copied"), sem("post_mul")
        rt_turned, rt_ready = sem("rt_turned"), sem("rt_ready")
        rr_step, rr_ready, rv_ready, rg_ready, rsg_ready, rgs_ready = (
            sem("rr_step"), sem("rr_ready"), sem("rv_ready"), sem("rg_ready"), sem("rsg_ready"), sem("rgs_ready"))
        rs_done, rpt_ready, ro_done, gn_step, gn_std, gn_ready, rn_ready, ry_ready, yt_done, yh_ready, yl_ready = (
            sem("rs_done"), sem("rpt_ready"), sem("ro_done"), sem("gn_step"), sem("gn_std"), sem("gn_ready"),
            sem("rn_ready"), sem("ry_ready"), sem("yt_done"), sem("yh_ready"), sem("yl_ready"))
        ss_done, fin_step, fin_std, o_scaled, o_ready, out_done = (
            sem("ss_done"), sem("fin_step"), sem("fin_std"), sem("o_scaled"), sem("o_ready"), sem("out_done"))

        CLASSES = [1, 4, 4]

        def token_block(ap, g, b):
            c = CLASSES[g]
            if c == 1:
                return ap[:, b * P:(b + 1) * P]
            v = ap.rearrange("p (l c) -> p c l", c=c)
            return v[:, b, :]

        def by_class(ap, g):
            return ap.rearrange("p (l c) -> p c l", c=CLASSES[g])

        def classes_of(ap, g):
            return ap.rearrange("p (c l) -> p c l", c=CLASSES[g])

        def by_step(ap, g):
            return ap.rearrange("p (c l) -> p l c", c=CLASSES[g])

        def steps_of(ap, g):
            return ap.rearrange("p (l c) -> p l c", c=CLASSES[g])

        def dilated_items(g):
            if g == 0:
                segs = [[(0, [0], 0), (1, [0, 1], P)], [(2, [1, 2], 0), (3, [2, 3], 2 * P)]]
            else:
                segs = [[(b, [b], b * P) for b in range(TB)]]
            return [(h, s) for h in range(8) for s in segs]

        FORGET_ITEMS = [(h, [(b, list(range(b + 1)), 0)]) for h in range(8) for b in range(TB)]
        ITEMS_A = [dilated_items(g) for g in range(3)]
        BODIES = [(g, half) for g in range(3) for half in range(2)]
        ITEM0, SEG0 = [], []
        n = m = 0
        for g, half in BODIES:
            ITEM0.append(n)
            SEG0.append(m)
            n += len(ITEMS_A[g])
            m += sum(len(s) for _, s in ITEMS_A[g])
        for half in range(2):
            ITEM0.append(n)
            n += len(FORGET_ITEMS)
        ITEM0.append(n)

        def width(segs):
            return segs[-1][2] + P * len(segs[-1][1])

        def rstd_col(g, b):
            return RB[:, T + 4 * g + b:T + 4 * g + b + 1]

        U = START
        PT0 = [0, 512, 896, 1152]
        rr_bn, gn_r = sem("rr_bn"), sem("gn_r")
        e_done, st_hi, st_lo, sel_ready = sem("e_done"), sem("st_hi"), sem("st_lo"), sem("sel_ready")
        gv_ready, post_sq, fold_step = sem("gv_ready"), sem("post_sq"), sem("fold_step")

        def own_banks(h):
            return 4 * (h % 2)

        body_banks = own_banks

        block = ctx.enter_context(nc.Block())

        @block.sync
        def _(sp):
            sp.dma_start(XTOK[:, :, :], x.rearrange("(b p) d -> p b d", p=P)).then_inc(x_in, 16)
            sp.dma_start(CST[:, :], cst).then_inc(consts_in, 16)
            sp.dma_start(VC[:, :], vec).then_inc(consts_in, 16)
            for u in range(UNITS):
                if u >= RING:
                    sp.wait_ge(hi_ready, u - RING + 1)
                    sp.wait_ge(lo_ready, u - RING + 1)
                sp.dma_start(WR[:, u % RING, :], ws[u]).then_inc(landed[u % RING], 16)
            for tb in range(TB):
                sp.wait_ge(o_ready, 2 * tb + 2)
                sp.dma_start(out[tb * P:(tb + 1) * P, :], OUT[:, tb, :]).then_inc(out_done, 16)
            sp.wait_ge(out_done, 16 * TB)

        @block.tensor
        def _(pe):
            def unit(u, kpair, hi, lo, bank, first, last, stationary, ready=None):
                s = u % RING
                pe.wait_ge(lo_ready, u + 1)
                for kk in range(2):
                    k = 2 * kpair + kk
                    if ready is not None:
                        ready(k)
                    for o in range(4):
                        if stationary:
                            cols = slice(kk * T + o * P, kk * T + (o + 1) * P)
                            pairs = [(WH[:, s, cols], hi[:, k, :]), (WH[:, s, cols], lo[:, k, :]),
                                     (WL[:, s, cols], hi[:, k, :])]
                        else:
                            cols = slice(kk * T, (kk + 1) * T)
                            xh, xl = stationary_x(hi, k, o), stationary_x(lo, k, o)
                            pairs = [(xh, WH[:, s, cols]), (xh, WL[:, s, cols]), (xl, WH[:, s, cols])]
                        for i, (l, r) in enumerate(pairs):
                            mm = pe.matmul(PS[:, bank + o, :], l, r, start=first and kk == 0 and i == 0,
                                           stop=last and kk == 1 and i == 2)
                mm.then_inc(unit_used, 1)

            order = [0]

            def stationary_x(t, k, o):
                return token_block(t[:, k, :], order[0], o)

            def group(u, kpairs, hi, lo, bank, stationary=True, ready=None, between=None):
                for j in range(kpairs):
                    unit(u + j, j, hi, lo, bank, j == 0, j == kpairs - 1, stationary, ready)
                    if between is not None and j in between:
                        between[j]()

            def statistics(s, bank, groups=()):
                pe.wait_ge(sq_sum, 7 * (s + 1) if s < 6 else 7 * s)
                mm = pe.matmul(PS[:, bank, :], ones, SQS[:, :], start=True, stop=True)
                for g in groups:
                    for b in range(TB):
                        mm = pe.matmul(PS[:, bank + 1, 4 * g + b:4 * g + b + 1], token_block(SQS[:, :], g, b),
                                       ones[:, 0:1], start=True, stop=True)
                mm.then_inc(stat_done, 1)

            def x_ready(v):
                def wait(k):
                    pe.wait_ge(x_hi, 8 * v + k + 1)
                    pe.wait_ge(x_lo, 8 * v + k + 1)
                return wait

            def attention(items, item0, own, values_ready, Q, K, V, PR, PT, forget=None):
                other = 4 - own
                N = len(items)
                for n in range(N + 3):
                    if n < N:
                        h, segs = items[n]
                        rows = slice(HD * (h % 2), HD * (h % 2) + HD)
                        if n >= 2:
                            pe.wait_ge(max_done, item0 + n - 1)
                        if forget is not None and n == 0:
                            forget(0)
                        for qb, kbs, c in segs:
                            mm = pe.matmul(PS[:, other + n % 2, c:c + P * len(kbs)],
                                           Q[rows, h // 2, qb * P:(qb + 1) * P],
                                           K[rows, h // 2, kbs[0] * P:(kbs[-1] + 1) * P], start=True, stop=True)
                        mm.then_inc(s_done, 1)
                        if forget is not None and n % TB == 1 and h < 7:
                            forget(h + 1)
                    m = n - 2
                    if 0 <= m < N:
                        h, segs = items[m]
                        pe.wait_ge(p_ready, item0 + m + 1)
                        if m >= 2:
                            pe.wait_ge(pt_copied, item0 + m - 1)
                        for c in range(0, width(segs), P):
                            mm = pe.transpose(PS[:, other + 2 + m % 2, c:c + P], PR[:, m % 3, c:c + P], ident)
                        mm.then_inc(t_done, 1)
                    m = n - 3
                    if 0 <= m < N:
                        h, segs = items[m]
                        rows = slice(HD * (h % 2), HD * (h % 2) + HD)
                        pe.wait_ge(pt_copied, item0 + m + 1)
                        if m == 0:
                            pe.wait_ge(v_ready, values_ready)
                        pair = h // 2
                        if pair >= 2 and h % 2 == 0:
                            pe.wait_ge(o_copied, PAIR0[0] + pair - 1)
                        for qb, kbs, c in segs:
                            for j, kb in enumerate(kbs):
                                mm = pe.matmul(PS[rows, own + pair % 2, qb * P:(qb + 1) * P],
                                               V[:, kb, h * HD:(h + 1) * HD],
                                               PT[:, m % 2, c + j * P:c + (j + 1) * P],
                                               start=j == 0, stop=j == len(kbs) - 1)
                        mm.then_inc(pv_done, 1)

            PAIR0 = [0]

            pe.wait_ge(x_in, 16)
            pe.wait_ge(consts_in, 32)
            for k in range(DT):
                for b in range(TB):
                    mm = pe.transpose(PS[:, k, b * P:(b + 1) * P], XTOK[:, b, k * P:(k + 1) * P], ident)
                mm.then_inc(x_turned, 1)

            pe.wait_ge(r_done, 8)
            for m, (g, half) in enumerate(BODIES):
                u = U["A"] + 12 * m
                own, other = body_banks(m), 4 - body_banks(m)
                order[0] = g
                group(u, 4, XH, XL, own, ready=x_ready(0),
                      between=None if m else {2: lambda: statistics(0, 6, (0, 1, 2))})
                if m:
                    pe.wait_ge(o_copied, 4 * m)
                pe.wait_ge(rb_var, 1)
                group(u + 4, 4, XH, XL, other)
                pe.wait_ge(rot_sh, 8 * m + 4)
                group(u + 8, 4, XH, XL, own, stationary=False)
                order[0] = 0
                pe.wait_ge(rot_sh, 8 * m + 8)
                pe.wait_ge(qk_ready, 8 * m + 8)
                PAIR0[0] = 4 * m
                attention(ITEMS_A[g], ITEM0[m], own, 4 * m + 4, A_Q, A_K, A_V, A_P, A_PT)
            pe.wait_ge(o_copied, 24)
            for g in range(3):
                for b in range(TB):
                    pe.transpose(PS[0:NH, g, b * P:(b + 1) * P], A_NM[:, g, :, b], ident)
                    mm = pe.transpose(PS[0:NH, 3 + g, b * P:(b + 1) * P], A_DEN[:, g, :, b], ident)
            mm.then_inc(st_turned, 1)
            pe.wait_ge(sel_ready, 1)
            pe.wait_ge(st_lo, 1)
            for t in range(DT):
                for g in range(3):
                    n = 3 * t + g
                    if n >= 8:
                        pe.wait_ge(bc_used, n - 7)
                    cols = slice(t * P, (t + 1) * P)
                    pe.matmul(PS[:, n % 8, :], A_SR[:, cols], A_MH[:, g, :], start=True, stop=False)
                    pe.matmul(PS[:, n % 8, :], A_SR[:, cols], A_ML[:, g, :], start=False, stop=True)\
                        .then_inc(bc_done, 1)
            pe.wait_ge(bc_used, 24)
            for d in range(2):
                group(U["AO"] + 4 * d, 4, XH, XL, 4 * d, ready=x_ready(1))

            def swiglu(layer, v, s):
                f, dn = U[f"F{layer}"], U[f"D{layer}"]
                for j in range(11):
                    n = 11 * layer + j
                    if j == 1:
                        pe.wait_ge(rb_var, s + 1)
                    if j >= 2:
                        pe.wait_ge(u_ready, n - 1)
                    group(f + 4 * j, 4, XH, XL, 4 if j % 2 == 0 else 0, ready=x_ready(v),
                          between=None if j else {1: lambda: statistics(s, 0)})
                pe.wait_ge(u_ready, 11 * layer + 10)

                def hidden(k):
                    pe.wait_ge(hh_ready, 11 * layer + k // 2 + 1)
                    pe.wait_ge(hl_ready, 11 * layer + k // 2 + 1)
                for d in range(2):
                    if d:
                        pe.wait_ge(u_ready, 11 * layer + 11)
                    group(dn + 11 * d, 11, HH, HL, 4 * d, ready=hidden)

            swiglu(0, 2, 1)

            u = U["BF"]
            pe.wait_ge(r_done, 21)
            pe.wait_ge(lo_ready, u + 1)
            for k in range(DT):
                x_ready(3)(k)
                cols = slice(k * P, (k + 1) * P)
                pe.matmul(PS[:, 4, :], WH[:, u % RING, cols], XH[:, k, :], start=k == 0, stop=False)
                pe.matmul(PS[:, 4, :], WH[:, u % RING, cols], XL[:, k, :], start=False, stop=False)
                mm = pe.matmul(PS[:, 4, :], WL[:, u % RING, cols], XH[:, k, :], start=False, stop=k == DT - 1)
            mm.then_inc(unit_used, 1)

            def broadcast_gate(half):
                def run(h):
                    n = 8 * half + h
                    if n >= 2:
                        pe.wait_ge(cb_ready, n - 1)
                    if h == 1:
                        pe.wait_ge(v_ready, 24 + 4 * half + 4)
                    pe.matmul(PS[:, body_banks(half) + 2 + h % 2, :], ident[0:NH, n:n + 1].to_broadcast([NH, P]), B_NC[:, :],
                              start=True, stop=True).then_inc(cb_done, 1)
                return run
            for half in range(2):
                u = U["B"] + 12 * half
                own, other = body_banks(half), 4 - body_banks(half)
                group(u, 4, XH, XL, own, between=None if half else {1: lambda: statistics(2, 6, (0,))})
                if half:
                    pe.wait_ge(o_copied, 28)
                    pe.wait_ge(cb_ready, 8)
                pe.wait_ge(rb_var, 3)
                pe.wait_ge(lf_step, 1)
                group(u + 4, 4, XH, XL, other)
                pe.wait_ge(bq_ready, 8 * half + 4)
                group(u + 8, 4, XH, XL, own, stationary=False)
                pe.wait_ge(bq_ready, 8 * half + 8)
                pe.wait_ge(v_ready, 24 + 4 * half + 3)
                pe.wait_ge(nc_ready, 1)
                PAIR0[0] = 24 + 4 * half
                attention(FORGET_ITEMS, ITEM0[6 + half], own, 24 + 4 * half + 4, B_Q, B_K, B_V, B_P, B_PT,
                          broadcast_gate(half))
            pe.wait_ge(o_copied, 32)
            pe.wait_ge(st_step, 8)
            for b in range(TB):
                mm = pe.transpose(PS[0:NH, 0, b * P:(b + 1) * P], B_DEN[:, :, b], ident)
            mm.then_inc(st_turned, 1)
            pe.wait_ge(st_z, 2)
            pe.wait_ge(sel_in, 32)
            for t in range(DT):
                if t >= 4:
                    pe.wait_ge(bc_used, 24 + t - 3)
                pe.matmul(PS[:, 4 + t % 4, :], B_SEL[:, t * P:(t + 1) * P], B_RD[:, :], start=True, stop=True).then_inc(bc_done, 1)
            for d in range(2):
                if d:
                    pe.wait_ge(bc_used, 32)
                group(U["BO"] + 4 * d, 4, XH, XL, 4 * d, ready=x_ready(4))
            swiglu(1, 5, 3)
            def two_norms():
                pe.wait_ge(sq_sum, 42)
                pe.matmul(PS[:, 6, :], ones, SQS[:, :], start=True, stop=True).then_inc(stat_done, 1)
                pe.matmul(PS[:, 7, :], ones, L_X[:, 1, :], start=True, stop=True).then_inc(stat_done, 1)
            for j in range(3):
                if j:
                    pe.wait_ge(xr_ready, 4 * j)
                group(U["L"] + 8 * j, 4, XH, XL, 0, ready=x_ready(6),
                      between=None if j else {3: two_norms})
                pe.wait_ge(rb_var, 6)
                if j:
                    pe.wait_ge(lg_ready, 4 * j)
                group(U["L"] + 8 * j + 4, 4, XH, XL, 4)
            pe.wait_ge(xr_ready, 12)
            pe.wait_ge(lg_ready, 12)
            for j in range(4):
                pe.wait_ge(ch_ready, 3 * j + 3)
                pe.wait_ge(cl_ready, 3 * j + 3)
                for which in range(2):
                    u = U["LG"] + 2 * j + which
                    s = u % RING
                    pe.wait_ge(lo_ready, u + 1)
                    if j:
                        pe.wait_ge(sig_done, 6 * (j - 1) + 3 * which + 3)
                    for o in range(3):
                        blocks = [(n, i) for n, (i, oo) in enumerate(GATE_BLOCKS) if oo == o]
                        for n, i in blocks:
                            cols = slice(n * P, (n + 1) * P)
                            b = PS[:, 4 * which + o, :]
                            pe.matmul(b, WH[:, s, cols], CH[:, 3 * j + i, :], start=n == blocks[0][0], stop=False)
                            pe.matmul(b, WH[:, s, cols], CL[:, 3 * j + i, :], start=False, stop=False)
                            mm = pe.matmul(b, WL[:, s, cols], CH[:, 3 * j + i, :], start=False,
                                           stop=n == blocks[-1][0])
                    mm.then_inc(unit_used, 1)
            pe.wait_ge(sig_done, 24)

            def recurrent(k):
                pe.wait_ge(ch_ready, LT + k + 1)
                pe.wait_ge(cl_ready, LT + k + 1)
            def post_sums(a, b):
                pe.wait_ge(lo_copied, 1)
                for k in range(a, b):
                    pe.wait_ge(post_sq, k + 1)
                    mm = pe.matmul(PS[:, 0, :], ones, L_G[:, k, :], start=k == 0, stop=k == DT - 1)
                return mm
            group(U["LO"], 6, CH, CL, 0, ready=recurrent)
            group(U["LO"] + 6, 6, CH, CL, 4, between={3: lambda: post_sums(0, 4)})
            post_sums(4, 8).then_inc(stat_done, 1)

            def outputs_turned(h):
                pe.wait_ge(rn_ready, 4 * h + 4)
                pe.wait_ge(ry_ready, 4 * h + 4)
                for j in range(4):
                    for b in range(TB):
                        mm = pe.transpose(PS[:, own_banks(h) + j, b * P:(b + 1) * P],
                                          R_G[:, b, j * P:(j + 1) * P], ident)
                    mm.then_inc(yt_done, 1)

            for h in range(RH):
                u = U["R"] + 12 * h
                own, other = own_banks(h), 4 - own_banks(h)
                group(u, 4, XH, XL, own, ready=x_ready(7),
                      between={1: lambda: outputs_turned(h - 1)} if h else {1: lambda: statistics(7, 6, (0,))})
                pe.wait_ge(rb_var, 8)
                if h:
                    pe.wait_ge(yl_ready, 4 * h)
                    pe.wait_ge(yh_ready, 4 * h)
                group(u + 4, 4, XH, XL, other, stationary=False)
                pe.wait_ge(rr_step, 4 * h + 4)
                group(u + 8, 4, XH, XL, own, stationary=False)
                pe.wait_ge(rr_ready, 4 * h + 4)
                pe.wait_ge(rsg_ready, 4 * h + 4)
                pe.wait_ge(rg_ready, 4 * h + 4)
                for kb in range(TB):
                    for c in range(2):
                        mm = pe.matmul(PS[:, other + kb, 0:T - kb * P], R_QK[:, 2 + c, kb * P:(kb + 1) * P],
                                       R_QK[:, c, kb * P:T], start=c == 0, stop=c == 1)
                    mm.then_inc(rs_done, 1)
                pe.wait_ge(rv_ready, 4 * h + 4)
                for qb in range(TB):
                    pe.wait_ge(rpt_ready, 4 * h + qb + 1)
                    for kb in range(qb + 1):
                        mm = pe.matmul(PS[:, own + qb, :],
                                       R_PT[:, PT0[kb] + (qb - kb) * P:PT0[kb] + (qb - kb + 1) * P],
                                       R_V[:, kb, :], start=kb == 0, stop=kb == qb)
                    mm.then_inc(ro_done, 1)

            def residual_turned():
                pe.wait_ge(yl_ready, 16)
                pe.wait_ge(yh_ready, 16)
                for b in range(TB):
                    if b >= 2:
                        pe.wait_ge(rt_ready, b - 1)
                    for k in range(DT):
                        mm = pe.transpose(PS[:, 4 + 2 * (b % 2) + k // 4, (k % 4) * P:(k % 4 + 1) * P],
                                          R[:, k, b * P:(b + 1) * P], ident)
                    mm.then_inc(rt_turned, 1)

            def heads_ready(k):
                pe.wait_ge(yl_ready, 4 * (k // 4) + 4)
                pe.wait_ge(yh_ready, 4 * (k // 4) + 4)
            group(U["RO"], 8, YH, YL, 0, stationary=False, ready=heads_ready,
                  between={1: lambda: outputs_turned(3), 4: residual_turned})
            pe.wait_ge(rt_ready, 4)
            group(U["RO"] + 8, 8, YH, YL, 4, stationary=False)

        @block.scalar
        def _(act):
            def split(a, b):
                for u in range(a, min(b, UNITS)):
                    s = u % RING
                    act.wait_ge(landed[s], 16 * (u // RING + 1))
                    if u >= RING:
                        act.wait_ge(unit_used, u - RING + 1)
                    nc.scalar.activation(WH[:, s, :], WR[:, s, :], ACT.Copy).then_inc(hi_ready, 1)

            def build_x(v, version, gain, before, ks=range(DT)):
                for k in ks:
                    act.wait_ge(r_done, 8 * version + k + 1)
                    if k == 0:
                        act.wait_ge(unit_used, before)
                    nc.scalar.activation(XH[:, k, :], R[:, k, :], ACT.Copy,
                                         scale=VC[:, VEC[gain] + k:VEC[gain] + k + 1]).then_inc(x_hi, 1)

            def root(s, width=T):
                act.wait_ge(rb_var, s + 1)
                nc.scalar.activation(RB[:, 0:width], RB[:, 0:width], ACT.Sqrt).then_inc(rb_std, 1)

            def exps(items, item0, PR, NM, DEN):
                for n, (h, segs) in enumerate(items):
                    act.wait_ge(nm_ready, item0 + n + 1)
                    for qb, kbs, c in segs:
                        w = slice(c, c + P * len(kbs))
                        e = nc.scalar.activation(PR[:, n % 3, w], PR[:, n % 3, w], ACT.Exp, bias=NM(h, qb),
                                                 accum_out=DEN(h, qb))
                    e.then_inc(p_ready, 1)

            act.dma_start(A_COS[:, :], turn_a[0]).then_inc(rota_in, 16)
            act.dma_start(A_SIN[:, :], turn_a[1]).then_inc(rota_in, 16)
            act.dma_start(A_SEL[:, :], sel).then_inc(sel_in, 16)
            act.wait_ge(consts_in, 32)
            for u in range(4):
                split(u, u + 1)
                build_x(0, 0, "a_norm", 0, range(2 * u, 2 * u + 2))
            split(4, 7)
            root(0, T + 12)
            for m, (g, half) in enumerate(BODIES):
                u = U["A"] + 12 * m
                split(u + 4 if m else 7, u + 16)
                act.wait_ge(unit_used, u + 12)
                act.wait_ge(rb_ready, 1)
                if m:
                    act.wait_ge(pv_done, ITEM0[m])
                for b in range(TB):
                    nc.scalar.activation(A_V[:, b, :], PS[:, body_banks(m) + b, :], ACT.Copy, scale=rstd_col(g, b))\
                        .then_inc(v_ready, 1)
                exps(ITEMS_A[g], ITEM0[m], A_P, lambda h, b: A_NM[:, g, 8 * half + h, b:b + 1],
                     lambda h, b: A_DEN[:, g, 8 * half + h, b:b + 1])
            act.wait_ge(pv_done, ITEM0[6])
            act.wait_ge(sel_in, 16)
            nc.scalar.activation(A_SR[:, :], A_SEL[:, :], ACT.Copy).then_inc(sel_ready, 1)
            act.wait_ge(st_step, 5)
            nc.scalar.activation(A_MN[:, :, :], A_MN[:, :, :], ACT.Exp).then_inc(st_exp, 1)
            act.wait_ge(st_z, 1)
            nc.scalar.activation(A_MH[:, :, :], A_MN[:, :, :], ACT.Copy).then_inc(st_hi, 1)
            for t in range(DT):
                act.wait_ge(y_sum, 2 * t + 2)
                nc.scalar.activation(XH[:, t, :], A_Y[:, t % 2, :], ACT.Copy).then_inc(x_hi, 1)
            split(U["AO"] + 4, U["AO"] + 8)

            def swiglu(layer, v, version, s, gain):
                f, dn = U[f"F{layer}"], U[f"D{layer}"]
                split(f, f + 4)
                build_x(v, version, gain, f)
                split(f + 4, f + 6)
                root(s)
                for j in range(11):
                    n = 11 * layer + j
                    split(f + 4 * j + (4 if j else 6), f + 4 * j + 8)
                    act.wait_ge(g_ready, n + 1)
                    if j:
                        act.wait_ge(gs_ready, n)
                    nc.scalar.activation(F_S[:, :, :], F_G[:, :, :], ACT.Sigmoid).then_inc(sg_ready, 1)
                    act.wait_ge(ht_ready, n + 1)
                    nc.scalar.activation(HH[:, 2 * j:2 * j + 2, :], F_U[:, :, :], ACT.Copy).then_inc(hh_ready, 1)
                split(dn + 4, dn + 15)

            swiglu(0, 2, 1, 1, "ffn0")

            d0 = U["D0"]
            build_x(3, 2, "b_norm", d0, range(0, 4))
            split(d0 + 15, d0 + 26)
            build_x(3, 2, "b_norm", d0, range(4, 8))
            split(U["BF"] + 4, U["BF"] + 7)
            root(2, T + 4)
            act.dma_start(B_SEL[:, :], sel).then_inc(sel_in, 16)
            split(U["BF"] + 7, U["BF"] + 9)
            act.wait_ge(lf_step, 3)
            nc.scalar.activation(B_E[:, :], B_A[:, :], ACT.Exp, scale=-1.0).then_inc(lf_exp, 1)

            def gate_copied(half, h):
                hh = 8 * half + h
                act.wait_ge(cb_done, hh + 1)
                if hh >= 2:
                    act.wait_ge(max_done, ITEM0[6] + TB * (hh - 1))
                nc.scalar.activation(B_CB[:, hh % 2, :], PS[:, body_banks(half) + 2 + h % 2, :], ACT.Copy)\
                    .then_inc(cb_ready, 1)
            for half in range(2):
                u = U["B"] + 12 * half
                split(u + (4 if half else 8), u + 16)
                act.wait_ge(unit_used, u + 12)
                act.wait_ge(rb_ready, 3)
                if half:
                    act.wait_ge(pv_done, ITEM0[7])
                for b in range(TB):
                    nc.scalar.activation(B_V[:, b, :], PS[:, body_banks(half) + b, :], ACT.Copy, scale=rstd_col(0, b))\
                        .then_inc(v_ready, 1)
                item0 = ITEM0[6 + half]
                for n, (h, segs) in enumerate(FORGET_ITEMS):
                    if n == 0:
                        gate_copied(half, 0)
                    act.wait_ge(nm_ready, item0 + n + 1)
                    qb, kbs, c = segs[0]
                    w = slice(0, P * len(kbs))
                    nc.scalar.activation(B_P[:, n % 3, w], B_P[:, n % 3, w], ACT.Exp,
                                         bias=B_NM[:, 8 * half + h, qb:qb + 1],
                                         accum_out=B_DEN[:, 8 * half + h, qb:qb + 1]).then_inc(p_ready, 1)
                    if n % TB == 1 and h < 7:
                        gate_copied(half, h + 1)
            for t in range(DT):
                act.wait_ge(bc_used, 24 + t + 1)
                nc.scalar.activation(XH[:, t, :], B_Q[:, t % 2, :], ACT.Copy).then_inc(x_hi, 1)
            split(U["BO"] + 4, U["BO"] + 8)
            swiglu(1, 5, 3, 3, "ffn1")

            split(U["D1"] + 15, U["D1"] + 26)
            act.wait_ge(gv_ready, 2)
            for k in range(DT):
                act.wait_ge(r_done, 32 + k + 1)
                if k == 0:
                    act.wait_ge(unit_used, U["F1"] + 44)
                nc.scalar.activation(XH[:, k, :], R[:, k, :], ACT.Copy, scale=GV[:, 1, k:k + 1]).then_inc(x_hi, 1)
            split(U["L"] + 4, U["L"] + 8)
            act.wait_ge(rb_var, 6)
            nc.scalar.activation(RB[:, 0:T], RB[:, 0:T], ACT.Sqrt).then_inc(rb_std, 1)
            nc.scalar.activation(L_X[:, 0, :], L_X[:, 0, :], ACT.Sqrt).then_inc(rb_std, 1)
            act.wait_ge(ls_step, 1)
            nc.scalar.activation(L_S[:, 1, :], L_S[:, 0, :], ACT.Exp, scale=-1.0).then_inc(ls_exp, 1)
            for j in range(3):
                u = U["L"] + 8 * j
                if j:
                    split(u + 4, u + 8)
                for o in range(4):
                    c = 4 * j + o
                    act.wait_ge(xr_ready, c + 1)
                    if c >= 2:
                        act.wait_ge(cl_ready, c - 1)
                    nc.scalar.activation(L_XC[:, c % 2, :], L_XR[:, c % 2, 3:T + 3], ACT.Identity,
                                         scale=VC[:, VEC["conv3"] + c:VEC["conv3"] + c + 1],
                                         bias=VC[:, VEC["conv_b"] + c:VEC["conv_b"] + c + 1]).then_inc(xc_ready, 1)
                    act.wait_ge(conv_step, 3 * c + 3)
                    nc.scalar.activation(CH[:, c, :], L_XC[:, c % 2, :], ACT.Copy).then_inc(ch_ready, 1)
                split(u + 8, u + 12)
                for o in range(4):
                    c = 4 * j + o
                    act.wait_ge(lg_ready, c + 1)
                    if c >= 2:
                        act.wait_ge(lgs_ready, c - 1)
                    nc.scalar.activation(L_SG[:, c % 2, :], L_G[:, c, :], ACT.Sigmoid).then_inc(lsg_ready, 1)
            act.wait_ge(ls_ready, 2)
            for j in range(5):
                i = j % 2
                if j < 4:
                    u = U["LG"] + 2 * j
                    if j == 0:
                        act.wait_ge(cl_ready, 12)
                        act.wait_ge(lgs_ready, 12)
                    if j >= 2:
                        act.wait_ge(y_done, j - 1)
                    for which, (dst, bias) in enumerate(((L_R2[i], "b_a"), (L_I2[i], "b_x"))):
                        act.wait_ge(unit_used, u + which + 1)
                        for o in range(3):
                            c = VEC[bias] + 3 * j + o
                            nc.scalar.activation(dst[:, o, :], PS[:, 4 * which + o, :], ACT.Sigmoid,
                                                 bias=VC[:, c:c + 1]).then_inc(sig_done, 1)
                    split(u + 4, u + 6)
                if j:
                    act.wait_ge(q_done, j)
                    nc.scalar.activation(L_E2[1 - i], L_E2[1 - i], ACT.Sqrt).then_inc(sqrt_done, 1)
                if j < 4:
                    act.wait_ge(sig_done, 6 * j + 3)
                    if j >= 2:
                        act.wait_ge(cl_ready, LT + 3 * (j - 1))
                    for o in range(3):
                        c = 3 * j + o
                        nc.scalar.activation(L_A2[i][:, o, :], L_R2[i][:, o, :], ACT.Exp, scale=L_S[:, 5, c:c + 1])\
                            .then_inc(ae_done, 1)
                    act.wait_ge(ae_done, 6 * j + 3)
                    for o in range(3):
                        c = 3 * j + o
                        nc.scalar.activation(L_R2[i][:, o, :], L_R2[i][:, o, :], ACT.Tanh, scale=L_S[:, 7, c:c + 1])\
                            .then_inc(ae_done, 1)
                else:
                    split(U["LO"] + 4, U["LO"] + 5)
                if j:
                    act.wait_ge(y_done, j)
                    for o in range(3):
                        nc.scalar.activation(CH[:, 3 * (j - 1) + o, :], L_A2[1 - i][:, o, :], ACT.Copy)\
                            .then_inc(ch_ready, 1)
            split(U["LO"] + 5, U["LO"] + 10)
            for d in range(2):
                act.wait_ge(unit_used, U["LO"] + 6 * (d + 1))
                if d == 0:
                    act.wait_ge(y_done, 4)
                for k in range(4 * d, 4 * d + 4):
                    nc.scalar.activation(L_G[:, k, :], PS[:, k, :], ACT.Square).then_inc(post_sq, 1)
                split(U["LO"] + 10, U["LO"] + 16) if d == 0 else None
            root(6)

            build_x(7, 6, "pre1", U["R"])
            act.wait_ge(post_mul, 8)
            act.dma_start(R_COS[:, :], turn_r[0]).then_inc(rotr_in, 16)
            act.dma_start(R_SIN[:, :], turn_r[1]).then_inc(rotr_in, 16)

            def outputs_high(h):
                for j in range(4):
                    act.wait_ge(yt_done, 4 * h + j + 1)
                    nc.scalar.activation(YH[:, 4 * h + j, :], PS[:, own_banks(h) + j, :], ACT.Copy)\
                        .then_inc(yh_ready, 1)
            for h in range(RH):
                u = U["R"] + 12 * h
                own, other = own_banks(h), 4 - own_banks(h)
                if h:
                    act.wait_ge(rpt_ready, 4 * h)
                else:
                    act.wait_ge(r_done, 56)
                act.dma_start(R_D[:, :], decay[h]).then_inc(decay_in, 16)
                split(u + 4, u + 6)
                if h:
                    outputs_high(h - 1)
                else:
                    root(7, T + 4)
                split(u + 6, u + 12)
                act.wait_ge(unit_used, u + 8)
                act.wait_ge(rb_ready, 8)
                act.wait_ge(rr_ready, 4 * h + 4)
                for b in range(TB):
                    nc.scalar.activation(R_G[:, b, :], PS[:, other + b, :], ACT.Copy, scale=rstd_col(0, b))\
                        .then_inc(rg_ready, 1)
                    if 4 * h + b >= 2:
                        act.wait_ge(rgs_ready, 4 * h + b - 1)
                    nc.scalar.activation(R_SG[:, b % 2, :], PS[:, other + b, :], ACT.Sigmoid,
                                         scale=rstd_col(0, b)).then_inc(rsg_ready, 1)
                split(u + 12, u + 15)
                act.wait_ge(unit_used, u + 12)
                if h:
                    act.wait_ge(ro_done, 4 * h)
                for b in range(TB):
                    nc.scalar.activation(R_V[:, b, :], PS[:, own + b, :], ACT.Copy, scale=rstd_col(0, b))\
                        .then_inc(rv_ready, 1)
                split(u + 15, u + 16)
                act.wait_ge(gn_step, 5 * h + 5)
                nc.scalar.activation(R_ST[:, 8:12], R_ST[:, 8:12], ACT.Sqrt).then_inc(gn_std, 1)
                act.wait_ge(gn_ready, h + 1)
                act.wait_ge(rgs_ready, 4 * h + 4)
                for b in range(TB):
                    if 4 * h + b >= 2:
                        act.wait_ge(ry_ready, 4 * h + b - 1)
                    nc.scalar.activation(R_SG[:, b % 2, :], PS[:, own + b, :], ACT.Identity,
                                         scale=R_ST[:, 12 + b:13 + b], bias=R_ST[:, 16 + b:17 + b])\
                        .then_inc(rn_ready, 1)
            split(U["RO"] + 4, U["RO"] + 6)
            outputs_high(3)
            act.wait_ge(yt_done, 16)
            act.dma_start(GAIN[:, :], post1.partition_broadcast(P)).then_inc(gain_in, 16)
            split(U["RO"] + 6, U["RO"] + 12)
            for d in range(2):
                act.wait_ge(unit_used, U["RO"] + 8 * (d + 1))
                for b in range(TB):
                    if 4 * d + b:
                        act.wait_ge(ss_done, 4 * d + b)
                    nc.scalar.activation(R_PT[:, 0:T], PS[:, 4 * d + b, :], ACT.Square,
                                         accum_out=R_ST[:, 4 * d + b:4 * d + b + 1]).then_inc(ss_done, 1)
                split(U["RO"] + 12, U["RO"] + 16) if d == 0 else None
            act.wait_ge(fin_step, 2)
            nc.scalar.activation(R_ST[:, 8:12], R_ST[:, 8:12], ACT.Sqrt).then_inc(fin_std, 1)

        @block.gpsimd
        def _(pool):
            def squares(s, src, ready, i=None):
                i = s if i is None else i
                for k in range(DT):
                    ready(k)
                    if k == 0:
                        if s:
                            pool.wait_ge(stat_done, s)
                        nc.gpsimd.tensor_tensor(SQS[:, :], src[:, 0, :], src[:, 0, :], ALU.mult).then_inc(sq_mul, 1)
                        continue
                    if 7 * i + k - 1:
                        pool.wait_ge(sq_sum, 7 * i + k - 1)
                    nc.gpsimd.tensor_tensor(SQT[:, :], src[:, k, :], src[:, k, :], ALU.mult).then_inc(sq_mul, 1)
                    pool.wait_ge(sq_mul, 8 * i + k + 1)
                    nc.gpsimd.tensor_tensor(SQS[:, :], SQS[:, :], SQT[:, :], ALU.add).then_inc(sq_sum, 1)

            def residual(version):
                return lambda k: pool.wait_ge(r_done, 8 * version + k + 1)

            squares(0, R, residual(0))
            pool.wait_ge(tab_ready, 2)
            for m, (g, half) in enumerate(BODIES):
                for j in range(8):
                    r = 8 * m + j
                    dst = (A_Q if j < 4 else A_K)[:, j % 4, :]
                    pool.wait_ge(rot_sh, r + 1)
                    nc.gpsimd.tensor_tensor(A_SH[:, r % 2, :], A_SH[:, r % 2, :], A_SIN[:, :], ALU.mult)\
                        .then_inc(rot_m, 1)
                    pool.wait_ge(rot_a, r + 1)
                    pool.wait_ge(rot_m, r + 1)
                    if m and j == 0:
                        pool.wait_ge(s_done, ITEM0[m])
                    nc.gpsimd.tensor_tensor(by_step(dst, g), steps_of(A_T1[:, r % 2, :], g),
                                            steps_of(A_SH[:, r % 2, :], g), ALU.add).then_inc(qk_ready, 1)
            for t in range(DT):
                for i in range(2):
                    pool.wait_ge(bc_used, 3 * t + 2 + i)
                    if i:
                        pool.wait_ge(y_sum, 2 * t + 1)
                    elif t >= 2:
                        pool.wait_ge(x_lo, 8 + t - 1)
                    a = A_U[:, 0, :] if i == 0 else A_Y[:, t % 2, :]
                    nc.gpsimd.tensor_tensor(A_Y[:, t % 2, :], a, A_U[:, 1 + i, :], ALU.add).then_inc(y_sum, 1)

            def swiglu(layer, s, version):
                squares(s, R, residual(version))
                for j in range(11):
                    n = 11 * layer + j
                    pool.wait_ge(gs_ready, n + 1)
                    pool.wait_ge(u_ready, n + 1)
                    nc.gpsimd.tensor_tensor(F_U[:, :, :], F_G[:, :, :], F_U[:, :, :], ALU.mult).then_inc(ht_ready, 1)

            swiglu(0, 1, 1)
            squares(2, R, residual(2))
            swiglu(1, 3, 3)
            pool.wait_ge(stat_done, 4)
            pool.wait_ge(gv_ready, 1)
            for k in range(DT):
                pool.wait_ge(r_done, 32 + k + 1)
                first, n, m = SQS if k == 0 else SQT, 32 + 2 * k, 28 + 2 * k - 2
                second = L_X[:, 1, :] if k == 0 else L_X[:, 2, :]
                if k == 1:
                    pool.wait_ge(sq_mul, 34)
                if k >= 2:
                    pool.wait_ge(sq_sum, m)
                nc.gpsimd.tensor_tensor(first[:, :], R[:, k, :], R[:, k, :], ALU.mult).then_inc(sq_mul, 1)
                pool.wait_ge(sq_mul, n + 1)
                nc.gpsimd.tensor_tensor(second, first[:, :], GV[:, 0, k:k + 1].to_broadcast([P, T]), ALU.mult)\
                    .then_inc(sq_mul, 1)
                if k:
                    nc.gpsimd.tensor_tensor(SQS[:, :], SQS[:, :], SQT[:, :], ALU.add).then_inc(sq_sum, 1)
                    pool.wait_ge(sq_mul, n + 2)
                    nc.gpsimd.tensor_tensor(L_X[:, 1, :], L_X[:, 1, :], L_X[:, 2, :], ALU.add).then_inc(sq_sum, 1)
            for c in range(LT):
                pool.wait_ge(lsg_ready, c + 1)
                nc.gpsimd.tensor_tensor(L_G[:, c, :], L_G[:, c, :], L_SG[:, c % 2, :], ALU.mult).then_inc(lgs_ready, 1)
            pool.wait_ge(cl_ready, 12)
            pool.wait_ge(ch_ready, 12)
            for j in range(4):
                if j:
                    pool.wait_ge(ix_done, j)
                else:
                    pool.wait_ge(lgs_ready, 12)
                tiles, i = slice(3 * j, 3 * j + 3), j % 2
                nc.gpsimd.tensor_tensor(L_X[:, :, :], CH[:, tiles, :].bitcast(F32), CL[:, tiles, :].bitcast(F32),
                                        ALU.add).then_inc(xs_done, 1)
                pool.wait_ge(xs_done, j + 1)
                pool.wait_ge(sig_done, 6 * j + 6)
                nc.gpsimd.tensor_tensor(L_I2[i], L_I2[i], L_X[:, :, :], ALU.mult).then_inc(ix_done, 1)
                pool.wait_ge(ae_done, 6 * j + 3)
                nc.gpsimd.tensor_tensor(L_E2[i], L_A2[i], L_A2[i], ALU.mult).then_inc(e_done, 1)
            squares(7, R, residual(6), 6)
            for h in range(RH):
                for j in range(4):
                    pair, i = divmod(j, 2)
                    pool.wait_ge(rr_step, 4 * h + 2 * pair + 2)
                    if h and j == 0:
                        pool.wait_ge(rs_done, 4 * h)
                    nc.gpsimd.tensor_tensor(R_QK[:, j, :], R_T[0][:, i, :], R_T[1][:, 1 - i, :],
                                            ALU.subtract if i == 0 else ALU.add).then_inc(rr_ready, 1)

        @block.vector
        def _(dve):
            tt, stt, ts = nc.vector.tensor_tensor, nc.vector.scalar_tensor_tensor, nc.vector.tensor_scalar

            def split(a, b):
                for u in range(a, min(b, UNITS)):
                    s = u % RING
                    dve.wait_ge(hi_ready, u + 1)
                    tt(WL[:, s, :], WR[:, s, :], WH[:, s, :].bitcast(F32), ALU.subtract).then_inc(lo_ready, 1)

            def x_low(v, gain, k):
                dve.wait_ge(x_hi, 8 * v + k + 1)
                dve.wait_ge(r_done, 8 * VERSION[v] + k + 1)
                stt(XL[:, k, :], R[:, k, :], VC[:, VEC[gain] + k:VEC[gain] + k + 1], XH[:, k, :].bitcast(F32),
                    ALU.mult, ALU.subtract).then_inc(x_lo, 1)

            VERSION = {0: 0, 2: 1, 3: 2, 5: 3, 6: 5, 7: 6}

            def r_inc(ins):
                ins.then_inc(r_done, 1)

            def variance(s, bank, width=T):
                dve.wait_ge(stat_done, s + 1)
                v = PS[:, bank:bank + 2, :].rearrange("p b t -> p (b t)")
                ts(RB[:, 0:width], v[:, 0:width], 1.0 / D, RMS_EPS, ALU.mult, ALU.add).then_inc(rb_var, 1)

            def rstd(s, width=T):
                dve.wait_ge(rb_std, s + 1)
                nc.vector.reciprocal(RB[:, 0:width], RB[:, 0:width]).then_inc(rb_ready, 1)
                dve.wait_ge(rb_ready, s + 1)

            def add_out(v, gain, end, unit_step, late=False):
                for d in range(2):
                    if d:
                        split(*unit_step[1])
                    else:
                        split(*unit_step[0])
                    dve.wait_ge(unit_used, end[d])
                    for k in range(4 * d, 4 * d + 4):
                        r_inc(tt(R[:, k, :], R[:, k, :], PS[:, k, :], ALU.add))
                        if gain and k % 4 and not late:
                            x_low(v, gain, k - 1)
                    if gain and not late:
                        x_low(v, gain, 4 * d + 3)
                for k in range(DT if gain and late else 0):
                    x_low(v, gain, k)

            def scores_max(n, item0, bank, segs, masks, PR, mx, nm):
                dve.wait_ge(s_done, item0 + n + 1)
                for qb, kbs, c in segs:
                    w = slice(c, c + P * len(kbs))
                    e = nc.vector.tensor_tensor_reduce(PR[:, n % 3, w], PS[:, bank + n % 2, w], masks(kbs), HD ** -0.5,
                                                       3 * MASKED, ALU.add, ALU.max, mx(qb))
                e.then_inc(max_done, 1)
                dve.wait_ge(max_done, item0 + n + 1)
                ts(nm(slice(segs[0][0], segs[-1][0] + 1)), mx(slice(segs[0][0], segs[-1][0] + 1)), -1.0, None,
                   ALU.mult).then_inc(nm_ready, 1)

            def attention_tail(items, n, item0, bank, PT, copy_out):
                m = n - 2
                if 0 <= m < len(items):
                    dve.wait_ge(t_done, item0 + m + 1)
                    if m >= 2:
                        dve.wait_ge(pv_done, item0 + m - 1)
                    w = width(items[m][1])
                    nc.vector.tensor_copy(PT[:, m % 2, 0:w], PS[:, bank + 2 + m % 2, 0:w]).then_inc(pt_copied, 1)
                m = n - 3
                if 0 <= m < len(items):
                    h = items[m][0]
                    if h % 2 and (m == len(items) - 1 or items[m + 1][0] != h):
                        dve.wait_ge(pv_done, item0 + m + 1)
                        copy_out(h // 2)

            dve.wait_ge(consts_in, 32)
            final, pre0 = VC[:, VEC["final"]:VEC["final"] + DT], VC[:, VEC["pre0"]:VEC["pre0"] + DT]
            tt(GV[:, 0, :], final, final, ALU.mult).then_inc(gv_ready, 1)
            tt(GV[:, 1, :], final, pre0, ALU.mult).then_inc(gv_ready, 1)

            for k in range(DT):
                dve.wait_ge(x_turned, k + 1)
                r_inc(nc.vector.tensor_copy(R[:, k, :], PS[:, k, :]))
            for u in range(4):
                split(u, u + 1)
                x_low(0, "a_norm", 2 * u)
                x_low(0, "a_norm", 2 * u + 1)
            split(4, 7)
            variance(0, 6, T + 12)
            rstd(0, T + 12)
            dve.wait_ge(rota_in, 32)
            tt(A_COS[:, :], A_COS[:, :], RB[:, 0:T], ALU.mult).then_inc(tab_ready, 1)
            tt(A_SIN[:, :], A_SIN[:, :], RB[:, 0:T], ALU.mult).then_inc(tab_ready, 1)
            dve.wait_ge(tab_ready, 2)
            swap = list(range(8, 16)) + list(range(8)) + list(range(16, 32))

            for m, (g, half) in enumerate(BODIES):
                u = U["A"] + 12 * m
                banks = own, other = body_banks(m), 4 - body_banks(m)
                for part in range(2):
                    split(max(7, u + 4 + 4 * part), u + 8 + 4 * part)
                    dve.wait_ge(unit_used, u + 4 + 4 * part)
                    for j in range(4):
                        r = 8 * m + 4 * part + j
                        if r >= 2:
                            dve.wait_ge(qk_ready, r - 1)
                        tt(A_T1[:, r % 2, :], PS[:, banks[part] + j, :], A_COS[:, :], ALU.mult).then_inc(rot_a, 1)
                        nc.vector.stream_shuffle(A_SH[:, r % 2, :], PS[:, banks[part] + j, :], swap).then_inc(rot_sh, 1)
                split(u + 12, u + 16)
                items, item0 = ITEMS_A[g], ITEM0[m]

                def copy_out(t):
                    nc.vector.tensor_copy(by_class(A_O[:, g, 4 * half + t, :], g), classes_of(PS[:, own + t % 2, :], g))\
                        .then_inc(o_copied, 1)

                def masks(kbs):
                    if g == 0:
                        return CST[:, BAND + P * (2 - len(kbs)):BAND + 2 * P]
                    return CST[:, BAND + P:BAND + 2 * P] if g == 1 else CST[:, CLASS:CLASS + P]
                for n in range(len(items) + 4):
                    if n < len(items):
                        h, segs = items[n]
                        hh = 8 * half + h
                        scores_max(n, item0, other, segs, masks, A_P,
                                   lambda b: A_MX[:, g, hh, b] if isinstance(b, slice) else A_MX[:, g, hh, b:b + 1],
                                   lambda b: A_NM[:, g, hh, b])
                    attention_tail(items, n, item0, other, A_PT, copy_out)
            dve.wait_ge(st_turned, 1)
            for g in range(3):
                nc.vector.tensor_copy(by_class(A_MN[:, g, :], g), classes_of(PS[0:NH, g, :], g)).then_inc(st_copied, 1)
                nc.vector.tensor_copy(by_class(A_DN[:, g, :], g), classes_of(PS[0:NH, 3 + g, :], g))\
                    .then_inc(st_copied, 1)
            dve.wait_ge(st_copied, 6)
            tt(A_M[:, :], A_MN[:, 0, :], A_MN[:, 1, :], ALU.min).then_inc(st_step, 1)
            dve.wait_ge(st_step, 1)
            tt(A_M[:, :], A_M[:, :], A_MN[:, 2, :], ALU.min).then_inc(st_step, 1)
            dve.wait_ge(st_step, 2)
            for g in range(3):
                tt(A_MN[:, g, :], A_M[:, :], A_MN[:, g, :], ALU.subtract).then_inc(st_step, 1)
            dve.wait_ge(st_exp, 1)
            tt(A_DN[:, :, :], A_DN[:, :, :], A_MN[:, :, :], ALU.mult).then_inc(st_step, 1)
            dve.wait_ge(st_step, 6)
            tt(A_Z[:, :], A_DN[:, 0, :], A_DN[:, 1, :], ALU.add).then_inc(st_step, 1)
            dve.wait_ge(st_step, 7)
            tt(A_Z[:, :], A_Z[:, :], A_DN[:, 2, :], ALU.add).then_inc(st_copied, 1)
            dve.wait_ge(st_copied, 7)
            nc.vector.reciprocal(A_M[:, :], A_Z[:, :]).then_inc(st_copied, 1)
            dve.wait_ge(st_copied, 8)
            tt(A_MN[:, :, :], A_MN[:, :, :], A_M[:, :].unsqueeze(1).to_broadcast([NH, 3, T]), ALU.mult)\
                .then_inc(st_z, 1)
            dve.wait_ge(st_hi, 1)
            tt(A_ML[:, :, :], A_MN[:, :, :], A_MH[:, :, :].bitcast(F32), ALU.subtract).then_inc(st_lo, 1)
            for t in range(DT):
                for g in range(3):
                    n = 3 * t + g
                    dve.wait_ge(bc_done, n + 1)
                    if t:
                        dve.wait_ge(y_sum, 2 * t - 1 if g < 2 else 2 * t)
                    tt(A_U[:, g, :], A_O[:, g, t, :], PS[:, n % 8, :], ALU.mult).then_inc(bc_used, 1)
                if t:
                    dve.wait_ge(x_hi, 8 + t)
                    tt(XL[:, t - 1, :], A_Y[:, (t - 1) % 2, :], XH[:, t - 1, :].bitcast(F32), ALU.subtract)\
                        .then_inc(x_lo, 1)
            dve.wait_ge(x_hi, 16)
            tt(XL[:, 7, :], A_Y[:, 1, :], XH[:, 7, :].bitcast(F32), ALU.subtract).then_inc(x_lo, 1)
            ao = U["AO"]
            add_out(2, "ffn0", (ao + 4, ao + 8), ((ao + 4, ao + 8), (ao + 8, ao + 12)), True)

            def swiglu(layer, s):
                f, dn = U[f"F{layer}"], U[f"D{layer}"]
                split(f + 4, f + 6)
                variance(s, 0)
                rstd(s)
                rb2 = RB[:, 0:T].unsqueeze(1).to_broadcast([P, 2, T])

                def low(j):
                    dve.wait_ge(hh_ready, 11 * layer + j + 1)
                    tt(HL[:, 2 * j:2 * j + 2, :], F_U[:, :, :], HH[:, 2 * j:2 * j + 2, :].bitcast(F32),
                       ALU.subtract).then_inc(hl_ready, 1)
                for j in range(11):
                    n = 11 * layer + j
                    bank = 4 if j % 2 == 0 else 0
                    u = f + 4 * j
                    if j:
                        split(u + 4, u + 6)
                        low(j - 1)
                    split(u + 6, u + 8)
                    dve.wait_ge(unit_used, u + 4)
                    tt(F_G[:, :, :], PS[:, bank:bank + 2, :], rb2, ALU.mult).then_inc(g_ready, 1)
                    if j:
                        dve.wait_ge(hl_ready, n)
                    tt(F_U[:, :, :], PS[:, bank + 2:bank + 4, :], rb2, ALU.mult).then_inc(u_ready, 1)
                    dve.wait_ge(sg_ready, n + 1)
                    tt(F_G[:, :, :], F_G[:, :, :], F_S[:, :, :], ALU.mult).then_inc(gs_ready, 1)
                low(10)
                return dn

            dn = swiglu(0, 1)
            add_out(3, "b_norm", (dn + 11, dn + 22), ((dn + 4, dn + 15), (dn + 15, dn + 26)))

            split(U["BF"] + 4, U["BF"] + 7)
            variance(2, 6, T + 4)
            rstd(2, T + 4)
            dve.wait_ge(unit_used, U["BF"] + 1)
            tt(B_Z[:, :], PS[0:NH, 4, :], RB[0:NH, 0:T], ALU.mult).then_inc(lf_step, 1)
            split(U["BF"] + 7, U["BF"] + 9)
            count = [1]

            def step(ins):
                count[0] += 1
                ins.then_inc(lf_step, 1)
                dve.wait_ge(lf_step, count[0])
            dve.wait_ge(lf_step, 1)
            step(ts(B_Z[:, :], B_Z[:, :], VC[0:NH, VEC["b_f"]:VEC["b_f"] + 1], None, ALU.add))
            step(stt(B_A[:, :], B_Z[:, :], -1.0, B_Z[:, :], ALU.mult, ALU.max))
            dve.wait_ge(lf_exp, 1)

            def log1p_half(e, s, w, q, stp):
                stp(ts(w, e, 2.0, None, ALU.add))
                stp(nc.vector.reciprocal(w, w))
                stp(tt(s, e, w, ALU.mult))
                stp(tt(w, s, s, ALU.mult))
                stp(ts(q, w, 1.0 / 17, None, ALU.mult))
                for odd in (15, 13, 11, 9, 7, 5, 3):
                    stp(stt(q, q, 1.0 / odd, w, ALU.add, ALU.mult))
                stp(stt(q, q, 1.0, s, ALU.add, ALU.mult))
            log1p_half(B_E[:, :], B_S[:, :], B_W[:, :], B_A[:, :], step)
            step(ts(B_Z[:, :], B_Z[:, :], 0.0, None, ALU.min))
            step(stt(B_A[:, :], B_A[:, :], 2.0, B_Z[:, :], ALU.mult, ALU.subtract))
            step(ts(B_A[:, :], B_A[:, :], 8.0, None, ALU.mult))
            step(nc.vector.memset(B_1[:, :], 1.0))
            nc.vector.tensor_tensor_scan(B_NC[:, :], B_1[:, :], B_A[:, :], 0.0, ALU.mult, ALU.add)\
                .then_inc(nc_ready, 1)

            def masked_gate(hh):
                dve.wait_ge(cb_ready, hh + 1)
                tt(B_DG[:, hh % 2, :].rearrange("p (b t) -> p b t", b=TB),
                   B_CB[:, hh % 2, :].rearrange("p (b t) -> p b t", b=TB),
                   CST[:, BAND + P:BAND + 2 * P].unsqueeze(1).to_broadcast([P, TB, P]), ALU.add).then_inc(dg_ready, 1)

            for half in range(2):
                u = U["B"] + 12 * half
                banks = own, other = body_banks(half), 4 - body_banks(half)
                for part in range(2):
                    if half or part:
                        split(u + 4 + 4 * part, u + 8 + 4 * part)
                    dve.wait_ge(unit_used, u + 4 + 4 * part)
                    if half:
                        dve.wait_ge(s_done, ITEM0[7])
                    for j in range(4):
                        tt((B_K if part else B_Q)[:, j, :], PS[:, banks[part] + j, :], RB[:, 0:T], ALU.mult)\
                            .then_inc(bq_ready, 1)
                split(u + 12, u + 16)
                item0 = ITEM0[6 + half]

                def copy_out(t):
                    nc.vector.tensor_copy(B_O[:, 4 * half + t, :], PS[:, own + t % 2, :]).then_inc(o_copied, 1)
                for n in range(len(FORGET_ITEMS) + 4):
                    if n < len(FORGET_ITEMS):
                        h, segs = FORGET_ITEMS[n]
                        hh = 8 * half + h
                        qb = segs[0][0]
                        if n == 0:
                            masked_gate(hh)
                        if qb == 0:
                            dve.wait_ge(dg_ready, hh + 1)
                        dve.wait_ge(s_done, item0 + n + 1)
                        diag = slice(qb * P, (qb + 1) * P)
                        ttr = nc.vector.tensor_tensor_reduce
                        if qb:
                            w = slice(0, qb * P)
                            ttr(B_P[:, n % 3, w], PS[:, other + n % 2, w], B_CB[:, hh % 2, w], HD ** -0.5, 3 * MASKED,
                                ALU.add, ALU.max, B_MX[:, hh, qb, 1:2])
                        ttr(B_P[:, n % 3, diag], PS[:, other + n % 2, diag], B_DG[:, hh % 2, diag], HD ** -0.5, 3 * MASKED,
                            ALU.add, ALU.max, B_MX[:, hh, qb, 0:1]).then_inc(max_done, 1)
                        dve.wait_ge(max_done, item0 + n + 1)
                        if qb:
                            ts(B_NM[:, hh, qb:qb + 1], B_MX[:, hh, qb, 0:1], B_MX[:, hh, qb, 1:2], -1.0,
                               ALU.max, ALU.mult).then_inc(nm_ready, 1)
                        else:
                            ts(B_NM[:, hh, qb:qb + 1], B_MX[:, hh, qb, 0:1], -1.0, None, ALU.mult)\
                                .then_inc(nm_ready, 1)
                        if qb == 2 and h < 7:
                            masked_gate(hh + 1)
                    attention_tail(FORGET_ITEMS, n, item0, other, B_PT, copy_out)
            dve.wait_ge(p_ready, ITEM0[8])
            nc.vector.reciprocal(B_DEN[:, :, :], B_DEN[:, :, :]).then_inc(st_step, 1)
            dve.wait_ge(st_turned, 2)
            nc.vector.tensor_copy(B_RD[:, :], PS[0:NH, 0, :]).then_inc(st_z, 1)
            for t in range(DT):
                dve.wait_ge(bc_done, 24 + t + 1)
                if t >= 2:
                    dve.wait_ge(x_lo, 8 * 4 + t - 1)
                tt(B_Q[:, t % 2, :], B_O[:, t, :], PS[:, 4 + t % 4, :], ALU.mult).then_inc(bc_used, 1)
                dve.wait_ge(x_hi, 8 * 4 + t + 1)
                tt(XL[:, t, :], B_Q[:, t % 2, :], XH[:, t, :].bitcast(F32), ALU.subtract).then_inc(x_lo, 1)
            bo = U["BO"]
            add_out(5, "ffn1", (bo + 4, bo + 8), ((bo + 4, bo + 8), (bo + 8, bo + 12)), True)

            dn = swiglu(1, 3)
            add_out(None, None, (dn + 11, dn + 22), ((dn + 4, dn + 15), (dn + 15, dn + 26)))
            count = [0]

            def lstep(ins):
                count[0] += 1
                ins.then_inc(ls_step, 1)
                dve.wait_ge(ls_step, count[0])
            lam = VC[:, VEC["lam"]:VEC["lam"] + LT]
            nc.vector.memset(L_XR[:, :, 0:3], 0.0).then_inc(ls_ready, 1)
            dve.wait_ge(ls_ready, 1)
            for k in range(DT):
                dve.wait_ge(x_hi, 48 + k + 1)
                stt(XL[:, k, :], R[:, k, :], GV[:, 1, k:k + 1], XH[:, k, :].bitcast(F32), ALU.mult, ALU.subtract)\
                    .then_inc(x_lo, 1)
            lstep(stt(L_S[:, 0, :], lam, -1.0, lam, ALU.mult, ALU.max))
            split(U["L"] + 4, U["L"] + 8)
            dve.wait_ge(stat_done, 6)
            ts(L_X[:, 0, :], PS[:, 6, :], 1.0 / D, RMS_EPS, ALU.mult, ALU.add).then_inc(rb_var, 1)
            ts(RB[:, 0:T], PS[:, 7, :], 1.0 / D, None, ALU.mult).then_inc(fold_step, 1)
            dve.wait_ge(rb_var, 5)
            dve.wait_ge(fold_step, 1)
            stt(RB[:, 0:T], L_X[:, 0, :], RMS_EPS, RB[:, 0:T], ALU.mult, ALU.add).then_inc(rb_var, 1)
            rstd(4)

            def after_first_inputs():
                dve.wait_ge(rb_std, 6)
                nc.vector.reciprocal(L_X[:, 0, :], L_X[:, 0, :]).then_inc(rb_ready, 1)
                dve.wait_ge(rb_ready, 6)
                for k in range(DT):
                    c = VEC["final"] + k
                    r_inc(stt(R[:, k, :], R[:, k, :], VC[:, c:c + 1], L_X[:, 0, :], ALU.mult, ALU.mult))
                dve.wait_ge(ls_exp, 1)
                softplus()

            def softplus():
                log1p_half(L_S[:, 1, :], L_S[:, 2, :], L_S[:, 3, :], L_S[:, 4, :], lstep)
                lstep(ts(L_S[:, 2, :], lam, 0.0, None, ALU.min))
                lstep(stt(L_S[:, 3, :], L_S[:, 4, :], 2.0, L_S[:, 2, :], ALU.mult, ALU.subtract))
                lstep(ts(L_S[:, 5, :], L_S[:, 3, :], -8.0, None, ALU.mult))
                lstep(ts(L_S[:, 6, :], L_S[:, 3, :], -16.0, None, ALU.mult))
                ts(L_S[:, 7, :], L_S[:, 3, :], 8.0, None, ALU.mult).then_inc(ls_ready, 1)

            def convolve(c):
                for i in range(3):
                    dve.wait_ge(xc_ready, c + 1)
                    if i:
                        dve.wait_ge(conv_step, 3 * c + i)
                    w = VEC[f"conv{i}"] + c
                    stt(L_XC[:, c % 2, :], L_XR[:, c % 2, i:i + T], VC[:, w:w + 1], L_XC[:, c % 2, :],
                        ALU.mult, ALU.add).then_inc(conv_step, 1)

            def conv_low(c):
                dve.wait_ge(ch_ready, c + 1)
                tt(CL[:, c, :], L_XC[:, c % 2, :], CH[:, c, :].bitcast(F32), ALU.subtract).then_inc(cl_ready, 1)
            for j in range(3):
                u = U["L"] + 8 * j
                if j:
                    split(u + 4, u + 8)
                dve.wait_ge(unit_used, u + 4)
                for o in range(4):
                    c = 4 * j + o
                    tt(L_XR[:, c % 2, 3:T + 3], PS[:, o, :], RB[:, 0:T], ALU.mult).then_inc(xr_ready, 1)
                    if o:
                        convolve(c - 1)
                        conv_low(c - 1)
                convolve(4 * j + 3)
                conv_low(4 * j + 3)
                split(u + 8, u + 12)
                if j == 0:
                    after_first_inputs()
                dve.wait_ge(unit_used, u + 8)
                for o in range(4):
                    tt(L_G[:, 4 * j + o, :], PS[:, 4 + o, :], RB[:, 0:T], ALU.mult).then_inc(lg_ready, 1)
            for j in range(5):
                i = j % 2
                if j < 4:
                    split(U["LG"] + 2 * j + 4, U["LG"] + 2 * j + 6)
                if j:
                    dve.wait_ge(ix_done, j)
                    dve.wait_ge(sqrt_done, j)
                    tt(L_I2[1 - i], L_I2[1 - i], L_E2[1 - i], ALU.mult).then_inc(bt_done, 1)
                    dve.wait_ge(bt_done, j)
                    for o in range(3):
                        nc.vector.tensor_tensor_scan(L_R2[1 - i][:, o, :], L_A2[1 - i][:, o, :], L_I2[1 - i][:, o, :],
                                                     0.0, ALU.mult, ALU.add).then_inc(h_done, 1)
                    dve.wait_ge(h_done, 3 * j)
                    dve.wait_ge(lgs_ready, LT)
                    tt(L_A2[1 - i], L_R2[1 - i], L_G[:, 3 * j - 3:3 * j, :], ALU.mult).then_inc(y_done, 1)
                    if j == 4:
                        split(U["LO"] + 4, U["LO"] + 5)
                    for o in range(3):
                        c = 3 * (j - 1) + o
                        dve.wait_ge(ch_ready, LT + c + 1)
                        tt(CL[:, c, :], L_A2[1 - i][:, o, :], CH[:, c, :].bitcast(F32), ALU.subtract)\
                            .then_inc(cl_ready, 1)
                if j < 4:
                    dve.wait_ge(ae_done, 6 * j + 6)
                    dve.wait_ge(e_done, j + 1)
                    stt(L_E2[i], L_E2[i], 1.0, L_R2[i], ALU.add, ALU.mult).then_inc(q_done, 1)
            split(U["LO"] + 5, U["LO"] + 10)
            for k in range(DT):
                if k == 0:
                    dve.wait_ge(cl_ready, 2 * LT)
                if k == 4:
                    split(U["LO"] + 10, U["LO"] + 16)
                dve.wait_ge(post_sq, k + 1)
                nc.vector.tensor_copy(L_O[:, k, :], PS[:, k, :]).then_inc(lo_copied, 1)
            variance(6, 0)
            rstd(6)
            for k in range(DT):
                c = VEC["post0"] + k
                stt(L_O[:, k, :], L_O[:, k, :], VC[:, c:c + 1], RB[:, 0:T], ALU.mult, ALU.mult).then_inc(post_mul, 1)
                dve.wait_ge(post_mul, k + 1)
                r_inc(tt(R[:, k, :], R[:, k, :], L_O[:, k, :], ALU.add))
                if k:
                    x_low(7, "pre1", k - 1)
            x_low(7, "pre1", 7)

            split(U["R"] + 4, U["R"] + 6)
            variance(7, 6, T + 4)
            rstd(7, T + 4)
            dve.wait_ge(rotr_in, 32)
            tt(R_COS[:, :], R_COS[:, :], RB[:, 0:T], ALU.mult).then_inc(tab_ready, 1)
            tt(R_SIN[:, :], R_SIN[:, :], RB[:, 0:T], ALU.mult).then_inc(tab_ready, 1)
            dve.wait_ge(tab_ready, 4)
            cos2 = R_COS[:, :].unsqueeze(1).to_broadcast([P, 2, T])
            sin2 = R_SIN[:, :].unsqueeze(1).to_broadcast([P, 2, T])

            def outputs_low(h):
                for j in range(4):
                    dve.wait_ge(yt_done, 4 * h + j + 1)
                    dve.wait_ge(yh_ready, 4 * h + j + 1)
                    tt(YL[:, 4 * h + j, :], PS[:, own_banks(h) + j, :], YH[:, 4 * h + j, :].bitcast(F32),
                       ALU.subtract).then_inc(yl_ready, 1)
            for h in range(RH):
                u = U["R"] + 12 * h
                own, other = own_banks(h), 4 - own_banks(h)
                if h:
                    split(u + 4, u + 6)
                    outputs_low(h - 1)
                split(u + 6, u + 8)
                dve.wait_ge(unit_used, u + 4)
                for pair in range(2):
                    if pair:
                        dve.wait_ge(rr_ready, 4 * h + 2)
                    elif h:
                        dve.wait_ge(yt_done, 4 * h)
                    pos = slice(own + 2 * pair, own + 2 * pair + 2)
                    tt(R_T[0][:, :, :], PS[:, pos, :], cos2, ALU.mult).then_inc(rr_step, 1)
                    tt(R_T[1][:, :, :], PS[:, pos, :], sin2, ALU.mult).then_inc(rr_step, 1)
                split(u + 8, u + 12)
                for b in range(TB):
                    dve.wait_ge(rsg_ready, 4 * h + b + 1)
                    dve.wait_ge(rg_ready, 4 * h + b + 1)
                    tt(R_G[:, b, :], R_G[:, b, :], R_SG[:, b % 2, :], ALU.mult).then_inc(rgs_ready, 1)
                split(u + 12, u + 16)
                dve.wait_ge(decay_in, 16 * (h + 1))
                for kb in range(TB):
                    dve.wait_ge(rs_done, 4 * h + kb + 1)
                    if h and kb == 0:
                        dve.wait_ge(ro_done, 4 * h)
                    w = T - kb * P
                    tt(R_PT[:, PT0[kb]:PT0[kb] + w], PS[:, other + kb, 0:w], R_D[:, 0:w], ALU.mult)\
                        .then_inc(rpt_ready, 1)
                for b in range(TB):
                    dve.wait_ge(ro_done, 4 * h + b + 1)
                    nc.vector.bn_stats(R_ST[:, 20 + 6 * b:26 + 6 * b], PS[:, own + b, :]).then_inc(gn_step, 1)
                    dve.wait_ge(gn_step, 5 * h + b + 1)
                    nc.vector.bn_aggr(R_ST[:, 2 * b:2 * b + 2], R_ST[:, 20 + 6 * b:26 + 6 * b]).then_inc(rr_bn, 1)
                dve.wait_ge(rr_bn, 4 * h + 4)
                st = R_ST[:, 0:8].rearrange("p (b i) -> p b i", i=2)
                ts(R_ST[:, 8:12], st[:, :, 1], GN_EPS, None, ALU.add).then_inc(gn_step, 1)
                dve.wait_ge(gn_std, h + 1)
                nc.vector.reciprocal(R_ST[:, 12:16], R_ST[:, 8:12]).then_inc(gn_r, 1)
                dve.wait_ge(gn_r, h + 1)
                stt(R_ST[:, 16:20], st[:, :, 0], -1.0, R_ST[:, 12:16], ALU.mult, ALU.mult).then_inc(gn_ready, 1)
                for b in range(TB):
                    dve.wait_ge(rn_ready, 4 * h + b + 1)
                    dve.wait_ge(rgs_ready, 4 * h + b + 1)
                    tt(R_G[:, b, :], R_G[:, b, :], R_SG[:, b % 2, :], ALU.mult).then_inc(ry_ready, 1)
            split(U["RO"] + 4, U["RO"] + 6)
            outputs_low(3)
            split(U["RO"] + 6, U["RO"] + 8)
            dve.wait_ge(ro_done, 16)
            for b in range(TB):
                dve.wait_ge(rt_turned, b + 1)
                bank = 4 + 2 * (b % 2)
                nc.vector.tensor_copy(OUT[:, b, :], PS[:, bank:bank + 2, :].rearrange("p b t -> p (b t)"))\
                    .then_inc(rt_ready, 1)
            split(U["RO"] + 8, U["RO"] + 12)
            dve.wait_ge(gain_in, 16)
            for d in range(2):
                for b in range(TB):
                    dve.wait_ge(ss_done, 4 * d + b + 1)
                    tt(R[:, 4 * d + b, :], PS[:, 4 * d + b, :], GAIN[:, T * d:T * d + T], ALU.mult)\
                        .then_inc(o_scaled, 1)
                if d == 0:
                    split(U["RO"] + 12, U["RO"] + 16)
            tt(R_ST[:, 8:12], R_ST[:, 0:4], R_ST[:, 4:8], ALU.add).then_inc(fin_step, 1)
            dve.wait_ge(fin_step, 1)
            ts(R_ST[:, 8:12], R_ST[:, 8:12], 1.0 / D, RMS_EPS, ALU.mult, ALU.add).then_inc(fin_step, 1)
            dve.wait_ge(fin_std, 1)
            nc.vector.reciprocal(R_ST[:, 12:16], R_ST[:, 8:12]).then_inc(fin_step, 1)
            dve.wait_ge(fin_step, 3)
            dve.wait_ge(o_scaled, 8)
            for b in range(TB):
                for d in range(2):
                    w = slice(T * d, T * d + T)
                    stt(OUT[:, b, w], R[:, 4 * d + b, :], R_ST[:, 12 + b:13 + b], OUT[:, b, w],
                        ALU.mult, ALU.add).then_inc(o_ready, 1)


def rotary_tables():
    f32 = np.float32
    pos = np.arange(T, dtype=f32)
    inv = f32(500000.0) ** (-np.arange(8, dtype=f32) * f32(2.0) / f32(16.0))
    ang = (pos[None, :] * inv[:, None]).astype(f32)
    cos, sin = np.ones((2, HD, T), f32), np.zeros((2, HD, T), f32)
    cos[:, 0:8] = cos[:, 8:16] = np.cos(ang)
    sin[:, 0:8], sin[:, 8:16] = -np.sin(ang), np.sin(ang)
    a = np.stack([cos.reshape(P, T), sin.reshape(P, T)])
    inv = f32(10000.0) ** (-np.arange(0, 256, 2, dtype=f32) / f32(256))
    ang = (pos[None, :] * inv[:, None]).astype(f32)
    return a, np.stack([np.cos(ang), np.sin(ang)]).astype(f32)


def constant_table():
    i = np.arange(P)
    c = np.zeros((P, NCST), np.float32)
    c[:, IDENT:IDENT + P] = np.eye(P)
    c[:, ONES:ONES + P] = 1.0
    q, k = i[:, None], i[None, :]
    c[:, BAND:BAND + P] = np.where(k >= q, 0.0, MASKED)
    c[:, BAND + P:BAND + 2 * P] = np.where(k <= q, 0.0, MASKED)
    c[:, CLASS:CLASS + P] = np.where((k <= q) & (k % 4 == q % 4), 0.0, MASKED)
    return c


def decay_table():
    g = 1.0 - 2.0 ** (-5.0 - np.arange(RH, dtype=np.float64))
    diff = np.arange(T)[None, :] - np.arange(P)[:, None]
    return np.where(diff >= 0, g[:, None, None] ** np.maximum(diff, 0) / 16.0, 0.0).astype(np.float32)


def units(w):
    k, n = w.shape
    return w.reshape(k // 256, 2, P, n // 512, 512).transpose(3, 0, 2, 1, 4).reshape(-1, P, UNIT)


def kernel(**inputs):
    import concourse.bacc as _bacc
    from concourse.bass_utils import run_bass_kernel_spmd as _run

    v = {k: np.asarray(a) for k, a in inputs.items()}
    f32 = np.float32

    def gate_up(i):
        w = v["ffn_w_gu"][i].reshape(D, 2, 11, 256)
        return np.ascontiguousarray(w.transpose(0, 2, 1, 3)).reshape(D, 22 * 256)

    a_in = v["a_w_in"][0].reshape(D, 3, 3, 2, 512).transpose(0, 1, 3, 2, 4).reshape(D, -1)
    b_in = v["b_w_in"][0][:, :3072].reshape(D, 3, 2, 512).transpose(0, 2, 1, 3).reshape(D, -1)
    forget = np.zeros((DT, P, P), f32)
    forget[:, :, :NH] = v["b_w_in"][0][:, 3072:].reshape(DT, P, NH)
    forget = forget.transpose(1, 0, 2).reshape(1, P, UNIT)
    l_in = v["lru_w_in_2"][0].reshape(D, 2, 3, 512).transpose(0, 2, 1, 3).reshape(D, -1)
    gates = np.zeros((4, 2, P, UNIT), f32)
    for j in range(4):
        for which, name in enumerate(("lru_w_a_2", "lru_w_x_2")):
            full = np.zeros((384, 384), f32)
            for b in range(4):
                full[96 * b:96 * b + 96, 96 * b:96 * b + 96] = v[name][0, 4 * j + b]
            for n, (i, o) in enumerate(GATE_BLOCKS):
                gates[j, which, :, n * P:(n + 1) * P] = full[i * P:(i + 1) * P, o * P:(o + 1) * P]
    rw = v["ret_w_in_2"][0]
    r_in = np.concatenate([np.concatenate([
        rw[:, 256 * h:256 * h + 256], rw[:, 1024 + 256 * h:1280 + 256 * h],
        rw[:, 4096 + 512 * h:4608 + 512 * h], rw[:, 2048 + 512 * h:2560 + 512 * h]], axis=1) for h in range(RH)],
        axis=1)
    ws = np.concatenate([
        units(a_in), units(v["a_w_out"][0]), units(gate_up(0)), units(v["ffn_w_down"][0]),
        forget, units(b_in), units(v["b_w_out"][0]), units(gate_up(1)), units(v["ffn_w_down"][1]),
        units(l_in), gates.reshape(8, P, UNIT), units(v["lru_w_out_2"][0]),
        units(r_in), units(v["ret_w_out_2"][0])])
    assert ws.shape[0] == UNITS

    vec = np.zeros((P, NVEC), f32)

    def column(name, a):
        a = a.reshape(-1, P).T
        vec[:, VEC[name]:VEC[name] + a.shape[1]] = a
    for name, a in (("a_norm", v["a_norm"][0]), ("ffn0", v["ffn_norm"][0]), ("b_norm", v["b_norm"][0]),
                    ("ffn1", v["ffn_norm"][1]), ("final", v["final_norm"]), ("pre0", v["norm_pre_2"][0]),
                    ("post0", v["norm_post_2"][0]), ("pre1", v["norm_pre_2"][1]), ("conv_b", v["lru_conv_b_2"][0]),
                    ("b_a", v["lru_b_a_2"][0]), ("b_x", v["lru_b_x_2"][0]), ("lam", v["lru_lambda_2"][0])):
        column(name, a)
    for i in range(4):
        column(f"conv{i}", v["lru_conv_w_2"][0, i])
    vec[:NH, VEC["b_f"]] = v["b_f"][0]
    turn_a, turn_r = rotary_tables()

    arrays = {"ws": ws, "x": v["x"][0], "vec": vec, "cst": constant_table(),
              "sel": np.repeat(np.eye(NH, dtype=f32), HD, axis=1), "turn_a": turn_a, "turn_r": turn_r,
              "decay": decay_table(), "post1": v["norm_post_2"][1]}
    arrays = {k: np.ascontiguousarray(a) for k, a in arrays.items()}
    nc = _bacc.Bacc("TRN2", target_bir_lowering=False, num_devices=1)
    args = [nc.dram_tensor(f"in_{k}", a.shape, F32, kind="ExternalInput").ap() for k, a in arrays.items()]
    shape = (T, D)
    args.append(nc.dram_tensor("out_0", shape, F32, kind="ExternalOutput").ap())
    program(nc, *args)
    r = _run(nc, [{f"in_{k}": a for k, a in arrays.items()}], core_ids=[0])
    return r.results[0]["out_0"].reshape(1, T, D)
```
